# Optimizing a Trainium2 kernel written in Bass

```python
import math
import jax, jax.numpy as jnp
from jax import lax
import numpy as np

D_MODEL = 1024
BATCH = 1
SEQ = 512
DEPTH = 1

EPS = 1e-6
CONV_WIDTH = D_MODEL
CONV_K = 3
N_HEADS = 8
HEAD_DIM = 128
N_KV_HEADS = 2
GROUP = N_HEADS // N_KV_HEADS
ATTN_WIDTH = N_HEADS * HEAD_DIM
KV_WIDTH = N_KV_HEADS * HEAD_DIM
IDX_HEADS = 8
IDX_DIM = 64
INDEX_TOPK = 256
Q_BLOCK = 128
ATTN_SCALE = HEAD_DIM ** -0.5
IDX_SCALE = IDX_DIM ** -0.5
IDX_W_SCALE = IDX_HEADS ** -0.5
ROPE_THETA = 500000.0
ROPE_FRACTION = 4
PEER_HEADS = 8
PEER_KEY_DIM = 256
PEER_HALF = PEER_KEY_DIM // 2
N_KEYS = 128
N_EXPERTS = N_KEYS * N_KEYS
PEER_TOPK = 16
TOKEN_BLOCK = 128

COL_SIZES = (
    CONV_WIDTH,
    CONV_WIDTH,
    CONV_WIDTH,
    ATTN_WIDTH,
    KV_WIDTH,
    KV_WIDTH,
    IDX_HEADS * IDX_DIM,
    IDX_DIM,
    IDX_HEADS,
    D_MODEL,
    D_MODEL,
)
IN_COLS = sum(COL_SIZES)
SPLIT_POINTS = [int(c) for c in np.cumsum(COL_SIZES)[:-1]]

kernel_name = "hybrid_shortconv_dsa_peer_block"

def rms_norm(x, g):
    xf = x.astype(jnp.float32)
    y = xf * lax.rsqrt(jnp.mean(xf * xf, axis=-1, keepdims=True) + EPS)
    return (y * g.astype(jnp.float32)).astype(x.dtype)

def partial_rope(x, pos):
    d = x.shape[-1]
    r = d // ROPE_FRACTION
    half = r // 2
    inv_freq = ROPE_THETA ** (-jnp.arange(half, dtype=jnp.float32) / half)
    ang = pos.astype(jnp.float32)[:, None] * inv_freq[None, :]
    cos = jnp.cos(ang)[:, None, :]
    sin = jnp.sin(ang)[:, None, :]
    xf = x.astype(jnp.float32)
    x1, x2, rest = xf[..., :half], xf[..., half:r], xf[..., r:]
    out = jnp.concatenate([x1 * cos - x2 * sin, x2 * cos + x1 * sin, rest], axis=-1)
    return out.astype(x.dtype)

def short_conv_mixer(b_gate, c_gate, xt, conv_w):
    seq = xt.shape[1]
    u = c_gate * xt
    up = jnp.pad(u, ((0, 0), (CONV_K - 1, 0), (0, 0)))
    conv = sum(conv_w[j] * up[:, j:j + seq] for j in range(CONV_K))
    return b_gate * conv

def to_blocks(t, nblk):
    b = t.shape[0]
    t = t.reshape((b, nblk, Q_BLOCK) + t.shape[2:])
    return jnp.moveaxis(t, 1, 0)

def dsa_attention(q, k, v, qi, ki, wi):
    b, seq = q.shape[0], q.shape[1]
    n_keys_visible = seq
    k_sel = min(INDEX_TOPK, n_keys_visible // 4)
    nblk = seq // Q_BLOCK
    key_pos = jnp.arange(n_keys_visible)
    gather = jax.vmap(lambda tb, ib: tb[ib])

    def attend_block(args):
        qb, qib, wib, t0 = args
        tq = t0 + jnp.arange(Q_BLOCK)
        dots = jnp.einsum('bqhd,bsd->bqhs', qib, ki) * IDX_SCALE
        iscore = jnp.einsum('bqh,bqhs->bqs', wib, jax.nn.relu(dots)).astype(jnp.float32)
        causal = key_pos[None, :] <= tq[:, None]
        iscore = jnp.where(causal[None], iscore, -jnp.inf)
        _, sel = lax.top_k(iscore, k_sel)
        valid = sel <= tq[None, :, None]
        ks = gather(k, sel)
        vs = gather(v, sel)
        qg = qb.reshape(b, Q_BLOCK, N_KV_HEADS, GROUP, HEAD_DIM)
        s = jnp.einsum('bqgnd,bqkgd->bqgnk', qg, ks).astype(jnp.float32) * ATTN_SCALE
        s = jnp.where(valid[:, :, None, None, :], s, -jnp.inf)
        p = jax.nn.softmax(s, axis=-1).astype(vs.dtype)
        o = jnp.einsum('bqgnk,bqkgd->bqgnd', p, vs)
        return o.reshape(b, Q_BLOCK, ATTN_WIDTH)

    starts = jnp.arange(nblk) * Q_BLOCK
    out = lax.map(attend_block, (to_blocks(q, nblk), to_blocks(qi, nblk),
                                 to_blocks(wi, nblk), starts))
    return jnp.moveaxis(out, 0, 1).reshape(b, seq, ATTN_WIDTH)

def peer_layer(xn, peer_wq, peer_k1, peer_k2, peer_u, peer_v):
    b, seq, d = xn.shape
    xt = xn.reshape(-1, TOKEN_BLOCK, d)

    def block(xc):
        q = (xc @ peer_wq).reshape(TOKEN_BLOCK, PEER_HEADS, 2, PEER_HALF)
        s1 = jnp.einsum('thd,hnd->thn', q[:, :, 0], peer_k1).astype(jnp.float32)
        s2 = jnp.einsum('thd,hnd->thn', q[:, :, 1], peer_k2).astype(jnp.float32)
        v1, i1 = lax.top_k(s1, PEER_TOPK)
        v2, i2 = lax.top_k(s2, PEER_TOPK)
        cand = (v1[..., :, None] + v2[..., None, :]).reshape(TOKEN_BLOCK, PEER_HEADS, PEER_TOPK * PEER_TOPK)
        cidx = (i1[..., :, None] * N_KEYS + i2[..., None, :]).reshape(TOKEN_BLOCK, PEER_HEADS, PEER_TOPK * PEER_TOPK)
        top_s, pos = lax.top_k(cand, PEER_TOPK)
        eidx = jnp.take_along_axis(cidx, pos, axis=-1)
        g = jax.nn.softmax(top_s, axis=-1)
        ue = peer_u[eidx]
        ve = peer_v[eidx]
        act = jax.nn.gelu(jnp.einsum('td,thkd->thk', xc, ue).astype(jnp.float32), approximate=False)
        return jnp.einsum('thk,thkd->td', (g * act).astype(ve.dtype), ve)

    out = lax.map(block, xt)
    return out.reshape(b, seq, d)

def setup_inputs(seed: int = 0) -> dict:
    key = jax.random.key(seed)
    ks = jax.random.split(key, 14)
    f32 = jnp.float32
    x = jax.random.normal(ks[0], (BATCH, SEQ, D_MODEL), f32)
    norm1_g = 1.0 + 0.02 * jax.random.normal(ks[1], (D_MODEL,), f32)
    w_in = jax.random.normal(ks[2], (D_MODEL, IN_COLS), f32) * D_MODEL ** -0.5
    conv_w = jax.random.normal(ks[3], (CONV_K, CONV_WIDTH), f32) * CONV_K ** -0.5
    q_norm_g = 1.0 + 0.02 * jax.random.normal(ks[4], (HEAD_DIM,), f32)
    k_norm_g = 1.0 + 0.02 * jax.random.normal(ks[5], (HEAD_DIM,), f32)
    w_o = jax.random.normal(ks[6], (D_MODEL, D_MODEL), f32) * D_MODEL ** -0.5
    norm2_g = 1.0 + 0.02 * jax.random.normal(ks[7], (D_MODEL,), f32)
    peer_wq = jax.random.normal(ks[8], (D_MODEL, PEER_HEADS * PEER_KEY_DIM), f32) * D_MODEL ** -0.5
    peer_k1 = jax.random.normal(ks[9], (PEER_HEADS, N_KEYS, PEER_HALF), f32) * PEER_HALF ** -0.5
    peer_k2 = jax.random.normal(ks[10], (PEER_HEADS, N_KEYS, PEER_HALF), f32) * PEER_HALF ** -0.5
    peer_u = jax.random.normal(ks[11], (N_EXPERTS, D_MODEL), f32) * D_MODEL ** -0.5
    peer_v = jax.random.normal(ks[12], (N_EXPERTS, D_MODEL), f32) * PEER_HEADS ** -0.5
    return {"x": x, "norm1_g": norm1_g, "w_in": w_in, "conv_w": conv_w,
            "q_norm_g": q_norm_g, "k_norm_g": k_norm_g, "w_o": w_o,
            "norm2_g": norm2_g, "peer_wq": peer_wq, "peer_k1": peer_k1,
            "peer_k2": peer_k2, "peer_u": peer_u, "peer_v": peer_v}

def reference(x, norm1_g, w_in, conv_w, q_norm_g, k_norm_g, w_o, norm2_g,
              peer_wq, peer_k1, peer_k2, peer_u, peer_v):
    b, seq, _ = x.shape
    pos = jnp.arange(seq)
    h = x
    for _layer in range(DEPTH):
        xn = rms_norm(h, norm1_g)
        proj = xn @ w_in
        (b_gate, c_gate, xt, q, k, v, qi, ki, wi, ga, gb) = jnp.split(proj, SPLIT_POINTS, axis=-1)
        y_a = short_conv_mixer(b_gate, c_gate, xt, conv_w)
        q = q.reshape(b, seq, N_HEADS, HEAD_DIM)
        k = k.reshape(b, seq, N_KV_HEADS, HEAD_DIM)
        v = v.reshape(b, seq, N_KV_HEADS, HEAD_DIM)
        q = partial_rope(rms_norm(q, q_norm_g), pos)
        k = partial_rope(rms_norm(k, k_norm_g), pos)
        qi = partial_rope(qi.reshape(b, seq, IDX_HEADS, IDX_DIM), pos)
        ki = partial_rope(ki.reshape(b, seq, 1, IDX_DIM), pos)[:, :, 0]
        wi = wi * IDX_W_SCALE
        y_b = dsa_attention(q, k, v, qi, ki, wi)
        merged = jax.nn.sigmoid(ga) * y_a + jax.nn.sigmoid(gb) * y_b
        h = h + merged @ w_o
        hn = rms_norm(h, norm2_g)
        h = h + peer_layer(hn, peer_wq, peer_k1, peer_k2, peer_u, peer_v)
    return h


_drawn_inputs = setup_inputs


def setup_inputs(seed=0):
    import zlib

    import numpy as np

    out = dict(_drawn_inputs(seed))
    spreads = {}
    factors = {'q_norm_g': 8.0, 'k_norm_g': 7.735, 'norm2_g': 2.699}
    for name, (base, spread) in spreads.items():
        noise = np.random.default_rng([zlib.crc32(name.encode()), seed]).standard_normal(out[name].shape)
        drawn = base * np.exp(spread * noise) if base else spread * noise
        out[name] = __import__('jax').numpy.asarray(drawn.astype(out[name].dtype))
    for name, factor in factors.items():
        out[name] = (out[name] * factor).astype(out[name].dtype)
    return out
```

```python
from contextlib import ExitStack

import concourse.bass as bass
from concourse import mybir

ALU = mybir.AluOpType
ACT = mybir.ActivationFunctionType
AX = mybir.AxisListType
F32 = mybir.dt.float32
U32 = mybir.dt.uint32

P = 128
SEQ, D = 512, 1024
NT = SEQ // P
KC = D // P
HEADS, HD, KVH = 8, 128, 2
GROUP = HEADS // KVH
IH, ID = 8, 64
TOPK_KEYS = min(256, SEQ // 4)
PH, NKEY, PTOP = 8, 128, 16
CONV_K = 3
EPS = 1e-6
ATTN_SCALE = HD ** -0.5
IDX_SCALE = ID ** -0.5
IDX_W_SCALE = IH ** -0.5
ROPE_Q, ROPE_I = HD // 4 // 2, ID // 4 // 2
MASKED = -1.0e30
TAKEN = -3.0e38
RING = 8
DIAGS = 4
UNITS = NT * HEADS
ITERS = NT * PH
CONST_COLS = 128 + 128 + 16 + 2 * NT * ROPE_Q + 2 * NT * ROPE_I
PARAM_COLS = KC + KC + KC * CONV_K


class Link:

    def __init__(self, eng, sem):
        self.eng, self.sem, self.count, self.var, self.per = eng, sem, 0, None, 0

    def __call__(self, ins):
        ins.then_inc(self.sem, 1)
        self.count += 1
        return self.count

    def upto(self, count):
        if self.var is None:
            self.eng.wait_ge(self.sem, count)
        else:
            self.eng.wait_ge(self.sem, self.var * self.per + count)
            self.eng.nop(nofuse=True)

    def then(self, ins):
        self.upto(self(ins))

    def enter(self, var, per):
        self.var, self.per, self.start = var, per, self.count

    def leave(self, trips):
        assert self.count - self.start == self.per, (self.count - self.start, self.per)
        self.count, self.var = self.start + trips * self.per, None


def build(nc, x, w_tok, w_small, w_chan, w_out, w_q, keys_t, uv, consts, params, rows, out):
    with ExitStack() as ctx:
        def sb(name, cols, dt=F32):
            return ctx.enter_context(nc.sbuf_tensor(name, [P, cols], dt))

        def sem(name):
            return ctx.enter_context(nc.semaphore(name))

        banks = ctx.enter_context(nc.psum_tensor("banks", [P, 8, 512], F32))
        resid = sb("resid", NT * D)[:].rearrange("p (b d) -> p b d", b=NT)
        tokmaj = sb("tokmaj", NT * D)[:]
        xn_tok = tokmaj.rearrange("p (b d) -> p b d", b=NT)
        gate_b = tokmaj.rearrange("p (m t) -> p m t", m=KC)
        xnT = sb("xnT", KC * SEQ)[:].rearrange("p (k t) -> p k t", k=KC)
        big = sb("big", (ITERS + 1) * 2 * NKEY)[:]
        scores = big
        chan_sets = big[:, 0:4 * 4 * SEQ].rearrange("p (s q t) -> p s q t", s=4, q=4)
        ring = sb("ring", RING * 2 * D)[:]
        slots = ring.rearrange("p (r e) -> p r e", r=RING)
        WSLOT = 5 * KC * P
        wslots = ring[:, 0:2 * WSLOT].rearrange("p (s e) -> p s e", s=2)
        raws = ring[:, 2 * WSLOT:2 * WSLOT + 2 * NT * 512].rearrange("p (s b c) -> p s b c", s=2, b=NT)
        tail = ring[:, 2 * WSLOT + 2 * NT * 512:]
        relus = tail[:, 0:2 * SEQ].rearrange("p (s t) -> p s t", s=2)
        probs = tail[:, 2 * SEQ:4 * SEQ].rearrange("p (s t) -> p s t", s=2)
        square = raws[:, 1, 0:2, :].rearrange("p b c -> p (b c)")
        UP = SEQ + CONV_K - 1
        u_pad = raws[:, 0, :, :].rearrange("p b c -> p (b c)")[:, 0:2 * UP].rearrange("p (s t) -> p s t", s=2)
        conv = raws[:, 0, :, :].rearrange("p b c -> p (b c)")[:, 2 * UP:2 * UP + SEQ]
        wo_sb = ring[:, 0:2 * KC * 512].rearrange("p (s k c) -> p s k c", s=2, k=KC)
        qreg = sb("qreg", HEADS * SEQ)[:]
        qT = qreg.rearrange("p (h t) -> p h t", h=HEADS)
        wq_sb = qreg.rearrange("p (s k c) -> p s k c", s=4, k=KC)
        kreg = sb("kreg", KVH * SEQ)[:]
        kT = kreg.rearrange("p (h t) -> p h t", h=KVH)
        q2T = kreg.rearrange("p (s t) -> p s t", s=2)
        vreg = sb("vreg", NT * KVH * HD)[:]
        v_tok = vreg.rearrange("p (b c) -> p b c", b=NT)
        key_sb = vreg[:, 0:4 * NKEY].rearrange("p (s n) -> p s n", s=4)
        ireg = sb("ireg", 4 * SEQ)[:]
        qiT = ireg.rearrange("p (h t) -> p h t", h=4)
        probsT = ireg[:, 0:2 * SEQ].rearrange("p (s t) -> p s t", s=2)
        g2row = ireg[:, 2 * SEQ:2 * SEQ + D]
        sc = ireg[:, 0:256].rearrange("p (a n) -> p a n", a=2)
        sc_cut = ireg[:, 256:512].rearrange("p (a n) -> p a n", a=2)
        cand = ireg[:, 512:768]
        cand_cut = ireg[:, 768:1024]
        onehot = ireg[:, 1024:1536].rearrange("p (a k n) -> p a k n", a=2, k=PTOP)
        diag = ireg[:, 1536:2048].rearrange("p (s n) -> p s n", s=DIAGS)
        kiT = sb("kiT", SEQ)[:]
        mreg = sb("mreg", KC * SEQ)[:]
        mixed = mreg.rearrange("p (m t) -> p m t", m=KC)
        head_sq = mreg[:, 0:NT * 512]
        turn = mreg[:, NT * 512:NT * 512 + 4 * NT * 4 * ROPE_Q].rearrange("p (q n) -> p q n", q=4)
        xcur = mreg[:, 0:2 * D].rearrange("p (s d) -> p s d", s=2)
        dotjunk = mreg[:, 2 * D:4 * D].rearrange("p (s d) -> p s d", s=2)
        mask_cols = [P * (b + 1) for b in range(NT)]
        mask_at = [sum(mask_cols[:b]) for b in range(NT)]
        maskreg = sb("maskreg", sum(mask_cols))[:]
        masks = [maskreg[:, mask_at[b]:mask_at[b] + mask_cols[b]] for b in range(NT)]
        cst = sb("cst", CONST_COLS)[:]
        ident, tri, iota = cst[:, 0:128], cst[:, 128:256], cst[:, 256:272]
        at = 272
        tables = []
        for half in (ROPE_Q, ROPE_Q, ROPE_I, ROPE_I):
            tables.append(cst[:, at:at + NT * half].rearrange("p (b r) -> p b r", b=NT))
            at += NT * half
        cos_q, sin_q, cos_i, sin_i = tables
        par = sb("par", PARAM_COLS)[:]
        g1, g2 = par[:, 0:KC], par[:, KC:2 * KC]
        taps = par[:, 2 * KC:].rearrange("p (m j) -> p m j", j=CONV_K)
        qk_gain = sb("qk_gain", 2 * HD)[:].rearrange("p (a c) -> p a c", a=2)
        wi = sb("wi", NT * IH)[:].rearrange("p (b h) -> p b h", b=NT)
        st = sb("st", 5 * 16)[:].rearrange("p (a n) -> p a n", a=5)
        mx8 = sb("mx8", 8)[:]
        sm = sb("sm", 8)[:].rearrange("p (s a) -> p s a", s=2)
        topv = sb("topv", 2 * PTOP)[:].rearrange("p (a k) -> p a k", a=2)
        topi = sb("topi", 2 * PTOP, U32)[:].rearrange("p (a k) -> p a k", a=2)
        topif = sb("topif", 2 * PTOP)[:].rearrange("p (a k) -> p a k", a=2)
        best = sb("best", PTOP)[:]
        pos = sb("pos", PTOP, U32)[:]
        posij = sb("posij", 2 * PTOP, U32)[:].rearrange("p (a k) -> p a k", a=2)
        posf = sb("posf", 2 * PTOP)[:].rearrange("p (a k) -> p a k", a=2)
        chosen = sb("chosen", 2 * PTOP)[:].rearrange("p (a k) -> p a k", a=2)
        eidx = sb("eidx", 2 * PTOP, U32)[:].rearrange("p (s k) -> p s k", s=2)
        gprob = sb("gprob", 2 * PTOP)[:].rearrange("p (s k) -> p s k", s=2)
        gstat = sb("gstat", 3)[:]
        dots = sb("dots", PTOP)[:]
        gel = sb("gel", PTOP)[:]

        const_in = sem("const_in")
        x_in = [sem(f"x_in{b}") for b in range(NT)]
        wtok_in = [sem(f"wtok_in{s}") for s in range(2)]
        wchan_in = [sem(f"wchan_in{s}") for s in range(2)]
        g2row_in = sem("g2row_in")
        wo_in = sem("wo_in")
        wq_in = [sem(f"wq_in{s}") for s in range(4)]
        n_sq = sem("n_sq")
        n_var = sem("n_var")
        n_root = sem("n_root")
        n_scaled = sem("n_scaled")
        n_turned = sem("n_turned")
        n_out = sem("n_out")
        tp_done = sem("tp_done")
        tp_out = sem("tp_out")
        tp_sq = sem("tp_sq")
        tp_ready = sem("tp_ready")
        tt_done = sem("tt_done")
        tt_out = sem("tt_out")
        id_done = sem("id_done")
        id_relu = sem("id_relu")
        id_used = sem("id_used")
        cp_done = sem("cp_done")
        cp_out = sem("cp_out")
        cv_done = sem("cv_done")
        s_done = sem("s_done")
        s_max = sem("s_max")
        s_exp = sem("s_exp")
        s_prob = sem("s_prob")
        p_turned = sem("p_turned")
        p_out = sem("p_out")
        o_done = sem("o_done")
        o_used = sem("o_used")
        y_done = sem("y_done")
        y_out = sem("y_out")
        xn_ready = sem("xn_ready")
        q_done = sem("q_done")
        q_out = sem("q_out")
        k_done = sem("k_done")
        k_out = sem("k_out")
        r_in = sem("r_in")
        r_max = sem("r_max")
        r_exp = sem("r_exp")
        r_done = sem("r_done")
        cur_in = sem("cur_in")
        row_in = [sem(f"row_in{s}") for s in range(RING)]
        dot_done = sem("dot_done")
        gel_done = sem("gel_done")
        diag_done = sem("diag_done")
        row_free = sem("row_free")
        acc_free = sem("acc_free")
        out_in = sem("out_in")
        part_out = sem("part_out")
        pad_set = sem("pad_set")
        ch_dve = sem("ch_dve")

        block = ctx.enter_context(nc.Block())
        TOKG = 4
        GH = [(0, 4), (4, 4), (0, 2)]
        TURNS = [4, 4, 2, 4, 1]
        TURN0 = [sum(TURNS[:g]) for g in range(5)]

        @block.sync
        def _(sp):
            sp.dma_start(cst, consts).then_inc(const_in, 16)
            for b in range(NT):
                sp.dma_start(resid[:, b, :], x[b * P:(b + 1) * P, :]).then_inc(x_in[b], 16)
                if b == 0:
                    sp.dma_start(par, params).then_inc(const_in, 16)
                    sp.dma_start(qk_gain[:, 0, :], rows[D:D + HD].partition_broadcast(P)).then_inc(const_in, 16)
                    sp.dma_start(qk_gain[:, 1, :], rows[D + HD:D + 2 * HD].partition_broadcast(P)).then_inc(const_in, 16)
            for g in range(TOKG + 1):
                if g >= 2:
                    sp.wait_ge(tp_done, NT * (g - 1))
                if g < TOKG:
                    sp.dma_start(wslots[:, g % 2, 0:KC * 512], w_tok[g]).then_inc(wtok_in[g % 2], 16)
                else:
                    sp.dma_start(wslots[:, g % 2, 0:KC * 72], w_small).then_inc(wtok_in[g % 2], 16)
            sp.wait_ge(tp_done, NT * TOKG)
            sp.dma_start(wslots[:, 1, :], w_chan[0]).then_inc(wchan_in[1], 16)
            sp.wait_ge(tp_done, NT * (TOKG + 1))
            sp.dma_start(wslots[:, 0, :], w_chan[1]).then_inc(wchan_in[0], 16)
            with sp.Fori(0, KC // 2 - 1) as mm:
                m = mm * 2
                for j in range(2):
                    sp.wait_ge(cp_done, m * 5 + 5 * (j + 1))
                    sp.dma_start(wslots[:, 1 - j, :], w_chan[bass.ds(m + (j + 2), 1)].rearrange("a p e -> p (a e)")).then_inc(wchan_in[1 - j], 16)
            sp.wait_ge(id_done, 8 * (NT - 1))
            sp.dma_start(g2row, rows[0:D].partition_broadcast(P)).then_inc(g2row_in, 16)
            sp.wait_ge(cp_done, 5 * KC)
            for s in range(2):
                sp.dma_start(wo_sb[:, s, :, :].rearrange("p k c -> p (k c)"), w_out[s]).then_inc(wo_in, 16)
            sp.wait_ge(s_done, UNITS)
            sp.wait_ge(o_done, UNITS)
            for s in range(4):
                sp.dma_start(wq_sb[:, s, :, :].rearrange("p k c -> p (k c)"), w_q[s]).then_inc(wq_in[s], 16)
                sp.dma_start(key_sb[:, s, :], keys_t[s]).then_inc(wq_in[s], 16)
            with sp.Fori(0, 2 * PH // 4 - 1) as jj:
                j = jj * 4
                for s in range(4):
                    sp.wait_ge(q_done, j + (s + 1))
                    sp.dma_start(wq_sb[:, s, :, :].rearrange("p k c -> p (k c)"), w_q[bass.ds(j + (s + 4), 1)].rearrange("a p e -> p (a e)")).then_inc(wq_in[s], 16)
                    sp.wait_ge(k_done, j + (s + 1))
                    sp.dma_start(key_sb[:, s, :], keys_t[bass.ds(j + (s + 4), 1)].rearrange("a p e -> p (a e)")).then_inc(wq_in[s], 16)
            sp.wait_ge(acc_free, 2 + ITERS)
            sp.dma_start(out.rearrange("(b p) d -> p b d", p=P), resid).then_inc(out_in, 16)
            sp.wait_ge(out_in, 16)

        @block.tensor
        def _(pe):
            def turn_blocks(first):
                for b in range(NT):
                    pe.wait_ge(n_scaled, first // 2 + b + 1)
                    for j in range(2):
                        m = first + 2 * b + j
                        if 2 * b + j >= 2:
                            pe.wait_ge(n_out, m - 1)
                        for c in range(4):
                            ins = pe.transpose(banks[:, 4 + j, c * P:(c + 1) * P],
                                               xn_tok[:, b, (4 * j + c) * P:(4 * j + c + 1) * P], ident)
                        ins.then_inc(n_turned, 1)

            pe.nop(nofuse=True).then_inc(row_free, RING)
            pe.wait_ge(const_in, 64)
            turn_blocks(0)

            def token_projection(g):
                pe.wait_ge(wtok_in[g % 2], 16 * (g // 2 + 1))
                cols = 512 if g < TOKG else 72
                w = wslots[:, g % 2, 0:KC * cols].rearrange("p (k c) -> p k c", k=KC)
                for b in range(NT):
                    n = NT * g + b
                    if g == 0:
                        pe.wait_ge(n_out, 2 * b + 2)
                    if n >= 4:
                        pe.wait_ge(tp_out, n - 3)
                    for k in range(KC):
                        ins = pe.matmul(banks[:, n % 4, 0:cols], xnT[:, k, b * P:(b + 1) * P], w[:, k, :],
                                        start=(k == 0), stop=(k == KC - 1))
                    ins.then_inc(tp_done, 1)

            def token_turns(g):
                pe.wait_ge(tp_ready, g + 1)
                for j in range(TURNS[g]):
                    m = TURN0[g] + j
                    if m >= 2:
                        pe.wait_ge(tt_out, m - 1)
                    for b in range(NT):
                        ins = pe.transpose(banks[:, 4 + m % 2, b * P:(b + 1) * P],
                                           raws[:, g % 2, b, j * P:(j + 1) * P], ident)
                    ins.then_inc(tt_done, 1)

            for g in range(TOKG + 2):
                if g <= TOKG:
                    token_projection(g)
                if g >= 1:
                    token_turns(g - 1)
            pe.wait_ge(tt_out, sum(TURNS))
            for b in range(1, NT):
                for h in range(IH):
                    n = IH * (b - 1) + h
                    if n >= 2:
                        pe.wait_ge(id_relu, n - 1)
                    rows64 = slice(64 * (h % 2), 64 * (h % 2) + 64)
                    pe.matmul(banks[:, 6 + n % 2, 0:mask_cols[b]], qiT[rows64, h // 2, b * P:(b + 1) * P],
                              kiT[rows64, 0:mask_cols[b]], start=True, stop=True).then_inc(id_done, 1)
            pe.wait_ge(tp_out, NT * (TOKG + 1))
            with pe.Fori(0, KC // 4) as mm:
                m = mm * 4
                for s in range(4):
                    slot = 1 - s % 2
                    pe.wait_ge(wchan_in[slot], m * 8 + 16 * (s // 2 + 1))
                    w = wslots[:, slot, :].rearrange("p (q k c) -> p q k c", q=5, k=KC)
                    for q in range(5):
                        n = 5 * s + q
                        pe.wait_ge(cp_out, m * 5 + (n + 1))
                        for k in range(KC):
                            ins = pe.matmul(banks[:, n % 4, :], w[:, q, k, :], xnT[:, k, :],
                                            start=(k == 0), stop=(k == KC - 1))
                        ins.then_inc(cp_done, 1)
            pe.wait_ge(cp_out, 4 + 5 * KC)
            for step in range(UNITS + 3):
                if step < UNITS:
                    b, h = divmod(step, HEADS)
                    if step >= 2:
                        pe.wait_ge(s_max, step - 1)
                    pe.matmul(banks[:, step % 2, 0:mask_cols[b]], qT[:, h, b * P:(b + 1) * P],
                              kT[:, h // GROUP, 0:mask_cols[b]], start=True, stop=True).then_inc(s_done, 1)
                n = step - 2
                if 0 <= n < UNITS:
                    b, h = divmod(n, HEADS)
                    pe.wait_ge(s_prob, n + 1)
                    if n >= 2:
                        pe.wait_ge(p_out, n - 1)
                    for c in range(b + 1):
                        ins = pe.transpose(banks[:, 4 + n % 2, c * P:(c + 1) * P], probs[:, n % 2, c * P:(c + 1) * P], ident)
                    ins.then_inc(p_turned, 1)
                n = step - 3
                if 0 <= n < UNITS:
                    b, h = divmod(n, HEADS)
                    pe.wait_ge(p_out, n + 1)
                    if n >= 2:
                        pe.wait_ge(o_used, n - 1)
                    g = h // GROUP
                    for c in range(b + 1):
                        ins = pe.matmul(banks[:, 2 + n % 2, 0:P], v_tok[:, c, g * HD:(g + 1) * HD],
                                        probsT[:, n % 2, c * P:(c + 1) * P], start=(c == 0), stop=(c == b))
                    ins.then_inc(o_done, 1)
            pe.wait_ge(wo_in, 32)
            pe.wait_ge(o_used, UNITS)
            for b in range(NT):
                for s in range(2):
                    n = 2 * b + s
                    if n >= 2:
                        pe.wait_ge(y_out, n - 1)
                    for k in range(KC):
                        ins = pe.matmul(banks[:, 6 + s, :], mixed[:, k, b * P:(b + 1) * P], wo_sb[:, s, k, :],
                                        start=(k == 0), stop=(k == KC - 1))
                    ins.then_inc(y_done, 1)
            turn_blocks(2 * NT)
            pe.wait_ge(n_out, 4 * NT)

            def query(j0, s):
                pe.wait_ge(wq_in[s], j0 * 8 + 32)
                pe.wait_ge(q_out, j0 + s + 1)
                for k in range(KC):
                    ins = pe.matmul(banks[:, s % 2, :], wq_sb[:, s, k, :], xnT[:, k, :], start=(k == 0), stop=(k == KC - 1))
                ins.then_inc(q_done, 1)

            def keyscore(j0, s):
                pe.wait_ge(q_out, j0 + s + 3)
                pe.wait_ge(k_out, j0 + s + 1)
                for b in range(NT):
                    ins = pe.matmul(banks[:, 2 + s % 2, b * P:(b + 1) * P], q2T[:, s % 2, b * P:(b + 1) * P],
                                    key_sb[:, s, :], start=True, stop=True)
                ins.then_inc(k_done, 1)

            with pe.Fori(0, 2 * PH // 4) as jj:
                j = jj * 4
                for s in range(5):
                    if s < 4:
                        query(j, s)
                    if s >= 1:
                        keyscore(j, s - 1)
            with pe.Fori(0, ITERS // 2) as ii:
                i = ii * 2
                for par2 in range(2):
                    pe.wait_ge(acc_free, i + (par2 + 1))
                    for k in range(PTOP):
                        n = PTOP * par2 + k
                        pe.wait_ge(diag_done, i * PTOP + (n + 1))
                        for s in range(2):
                            ins = pe.matmul(banks[:, 4 + 2 * par2 + s, :], diag[:, k % DIAGS, :],
                                            slots[:, k % RING, D + s * 512:D + (s + 1) * 512],
                                            start=(k == 0), stop=(k == PTOP - 1))
                        ins.then_inc(row_free, 1)
        @block.scalar
        def _(act):
            def squares(first, ready, count):
                for b in range(NT):
                    if ready is None:
                        act.wait_ge(x_in[b], 16)
                    else:
                        act.wait_ge(ready, count + 2 * b + 2)
                    if first + b >= 1:
                        act.wait_ge(n_sq, first + b)
                    act.activation(square, resid[:, b, :], ACT.Square, accum_out=st[:, 0, b:b + 1]).then_inc(n_sq, 1)

            def root(n, cols):
                act.wait_ge(n_var, n + 1)
                act.activation(st[:, 2, 0:cols], st[:, 1, 0:cols], ACT.Sqrt).then_inc(n_root, 1)

            squares(0, None, 0)
            root(0, NT)

            def copy_out(g):
                for b in range(NT):
                    n = NT * g + b
                    if b == 1 and 1 <= g <= 3:
                        root(g, 16 if g < 3 else 8)
                    act.wait_ge(tp_done, n + 1)
                    if b == 0 and g >= 2:
                        act.wait_ge(tt_done, TURN0[g - 2] + TURNS[g - 2])
                    if g == 0 and b == 0:
                        act.wait_ge(n_sq, NT)
                    if g == 2:
                        act.activation(raws[:, 0, b, 0:256], banks[:, n % 4, 0:256], ACT.Copy).then_inc(part_out, 1)
                        act.activation(v_tok[:, b, :], banks[:, n % 4, 256:512], ACT.Copy).then_inc(tp_out, 1)
                    elif g == 4:
                        act.activation(raws[:, 0, b, 0:64], banks[:, n % 4, 0:64], ACT.Copy).then_inc(part_out, 1)
                        act.activation(raws[:, 0, b, 64:128], banks[:, n % 4, 0:64], ACT.Copy).then_inc(part_out, 1)
                        act.activation(wi[:, b, :], banks[:, n % 4, 64:72], ACT.Copy, scale=IDX_W_SCALE).then_inc(tp_out, 1)
                    else:
                        act.activation(raws[:, g % 2, b, :], banks[:, n % 4, :], ACT.Copy).then_inc(tp_out, 1)

            def turns_out(g):
                for j in range(TURNS[g]):
                    m = TURN0[g] + j
                    act.wait_ge(tt_done, m + 1)
                    dst = {0: qT[:, j, :], 1: qT[:, 4 + j, :], 2: kT[:, j % 2, :], 3: qiT[:, j, :], 4: kiT}[g]
                    act.activation(dst, banks[:, 4 + m % 2, :], ACT.Copy).then_inc(tt_out, 1)

            for g in range(TOKG + 2):
                if g <= TOKG:
                    copy_out(g)
                if g >= 1:
                    turns_out(g - 1)
            for b in range(1, NT):
                for h in range(IH):
                    n = IH * (b - 1) + h
                    act.wait_ge(id_done, n + 1)
                    if n >= 2:
                        act.wait_ge(id_used, n - 1)
                    act.activation(relus[:, n % 2, 0:mask_cols[b]], banks[:, 6 + n % 2, 0:mask_cols[b]],
                                   ACT.Relu, scale=IDX_SCALE).then_inc(id_relu, 1)
            act.nop(nofuse=True).then_inc(cp_out, 4)
            act.wait_ge(n_scaled, NT)
            act.wait_ge(n_turned, 2 * NT)
            with act.Fori(0, KC // 4) as mm:
                m = mm * 4
                for s in range(4):
                    for q in range(5):
                        n = 5 * s + q
                        act.wait_ge(cp_done, m * 5 + (n + 1))
                        if q == 0:
                            act.wait_ge(cv_done, m + (s + 1))
                        act.nop(nofuse=True)
                        dst = chan_sets[:, s, q, :] if q < 4 else gate_b[:, bass.ds(m + s, 1), :].rearrange("p a t -> p (a t)")
                        act.activation(dst, banks[:, n % 4, :], ACT.Copy if q < 3 else ACT.Sigmoid).then_inc(cp_out, 1)
            for step in range(UNITS + 2):
                if step < UNITS:
                    b, h = divmod(step, HEADS)
                    act.wait_ge(s_max, step + 1)
                    act.activation(probs[:, step % 2, 0:mask_cols[b]], probs[:, step % 2, 0:mask_cols[b]], ACT.Exp,
                                   bias=sm[:, step % 2, 1:2], scale=ATTN_SCALE,
                                   accum_out=sm[:, step % 2, 2:3]).then_inc(s_exp, 1)
                n = step - 2
                if n >= 0:
                    b, h = divmod(n, HEADS)
                    act.wait_ge(p_turned, n + 1)
                    if n >= 2:
                        act.wait_ge(o_done, n - 1)
                    act.activation(probsT[:, n % 2, 0:mask_cols[b]], banks[:, 4 + n % 2, 0:mask_cols[b]], ACT.Copy).then_inc(p_out, 1)
            act.wait_ge(p_turned, UNITS)
            squares(NT, y_out, 0)
            root(4, NT)
            act.nop(nofuse=True).then_inc(q_out, 2)
            act.wait_ge(s_done, UNITS)
            with act.Fori(0, 2 * PH // 4) as jj:
                j = jj * 4
                for s in range(4):
                    act.wait_ge(q_done, j + (s + 1))
                    act.wait_ge(k_out, j + (s + 1))
                    act.nop(nofuse=True)
                    act.activation(q2T[:, s % 2, :], banks[:, s % 2, :], ACT.Copy).then_inc(q_out, 1)

            act.wait_ge(k_out, 2 + 2 * PH)
            act.wait_ge(xn_ready, NT)
            act.wait_ge(y_done, 2 * NT)
            act.wait_ge(pad_set, 1)
            act.activation(sc.rearrange("p a n -> p (a n)"), scores[:, 0:2 * NKEY], ACT.Copy).then_inc(r_in, 1)
            act.wait_ge(r_max, 1)
            act.activation(gprob[:, 0, :], best, ACT.Exp, bias=gstat[:, 0:1], accum_out=gstat[:, 1:2]).then_inc(r_exp, 1)
            with act.Fori(0, ITERS // 2) as ii:
                i = ii * 2
                for s in range(2):
                    act.nop(nofuse=True)
                    act.activation(xcur[:, s, :], xn_tok[:, bass.ds(i // PH, 1), :].rearrange("p a d -> p (a d)"), ACT.Copy).then_inc(cur_in, 1)
                    act.wait_ge(r_done, i + (s + 1))
                    act.nop(nofuse=True)
                    act.activation(sc.rearrange("p a n -> p (a n)"),
                                   scores[:, bass.ds((i + (s + 1)) * (2 * NKEY), 2 * NKEY)], ACT.Copy).then_inc(r_in, 1)
                    for q in range(4):
                        act.wait_ge(dot_done, i * PTOP + (PTOP * s + 4 * q + 4))
                        act.activation(gel[:, 4 * q:4 * q + 4], dots[:, 4 * q:4 * q + 4], ACT.Gelu).then_inc(gel_done, 1)
                        if q == 1:
                            act.wait_ge(r_max, i + (s + 2))
                            act.activation(gprob[:, 1 - s, :], best, ACT.Exp, bias=gstat[:, 0:1],
                                           accum_out=gstat[:, 1:2]).then_inc(r_exp, 1)

        @block.gpsimd
        def _(pool):
            pool.memset(scores[:, ITERS * 2 * NKEY:], 0.0).then_inc(pad_set, 1)
            pool.wait_ge(g2row_in, 16)
            for b in range(NT):
                pool.wait_ge(n_turned, 2 * NT + 2 * b + 2)
                pool.tensor_tensor(xn_tok[:, b, :], xn_tok[:, b, :], g2row, ALU.mult).then_inc(xn_ready, 1)
            with pool.Fori(0, ITERS // 2) as ii:
                i = ii * 2
                for s in range(2):
                    pool.wait_ge(r_done, i + (s + 1))
                    for k in range(PTOP):
                        pool.wait_ge(row_free, i * PTOP + (PTOP * s + k + 1))
                        pool.nop(nofuse=True)
                        pool.indirect_dma_start(slots[:, k % RING, :], None, uv,
                                                bass.IndirectOffsetOnAxis(eidx[:, s, k:k + 1], 0)).then_inc(row_in[k % RING], 16)

        @block.vector
        def _(dve):
            link = Link(dve, ch_dve)
            dve.wait_ge(const_in, 64)

            def inv_root(n, cols, width):
                dve.tensor_scalar(st[:, 1, 0:cols], st[:, 0, 0:cols], 1.0 / width, EPS, ALU.mult, ALU.add).then_inc(n_var, 1)
                dve.wait_ge(n_root, n + 1)
                link.then(dve.reciprocal(st[:, 3, 0:cols], st[:, 2, 0:cols]))
                link.then(dve.tensor_tensor(st[:, 4, 0:cols], st[:, 3, 0:cols], st[:, 3, 0:cols], ALU.mult))
                link.then(dve.tensor_tensor(st[:, 4, 0:cols], st[:, 4, 0:cols], st[:, 1, 0:cols], ALU.mult))
                link.then(dve.tensor_scalar(st[:, 4, 0:cols], st[:, 4, 0:cols], -0.5, 1.5, ALU.mult, ALU.add))
                link.then(dve.tensor_tensor(st[:, 3, 0:cols], st[:, 3, 0:cols], st[:, 4, 0:cols], ALU.mult))

            def norm_out(first, gain):
                for b in range(NT):
                    dve.tensor_scalar(xn_tok[:, b, :], resid[:, b, :], st[:, 3, b:b + 1], None, ALU.mult).then_inc(n_scaled, 1)
                for b in range(NT):
                    for j in range(2):
                        dve.wait_ge(n_turned, first + 2 * b + j + 1)
                        dve.tensor_tensor(xnT[:, 4 * j:4 * j + 4, b * P:(b + 1) * P],
                                          banks[:, 4 + j, :].rearrange("p (c t) -> p c t", c=4),
                                          gain[:, 4 * j:4 * j + 4].unsqueeze(2).to_broadcast([P, 4, P]),
                                          ALU.mult).then_inc(n_out, 1)

            dve.wait_ge(n_sq, NT)
            inv_root(0, NT, D)
            norm_out(0, g1)

            def rotate(x1, x2, cos, sin, shape):
                n = shape[1] * shape[2] * shape[3]
                c, s_ = (t.unsqueeze(2).to_broadcast(shape) for t in (cos, sin))
                tv = [turn[:, q, 0:n].rearrange("p (b h r) -> p b h r", b=shape[1], h=shape[2]) for q in range(4)]
                link(dve.tensor_tensor(tv[0], x1, c, ALU.mult))
                link(dve.tensor_tensor(tv[1], x2, s_, ALU.mult))
                link(dve.tensor_tensor(tv[2], x2, c, ALU.mult))
                link.then(dve.tensor_tensor(tv[3], x1, s_, ALU.mult))
                link(dve.tensor_tensor(x1, tv[0], tv[1], ALU.subtract))
                dve.tensor_tensor(x2, tv[2], tv[3], ALU.add).then_inc(tp_ready, 1)
                link.upto(link.count)

            for g in range(TOKG + 1):
                dve.wait_ge(tp_out, NT * (g + 1))
                if g == 2 or g == 4:
                    dve.wait_ge(part_out, NT if g == 2 else 3 * NT)
                if g <= 2:
                    nh = GH[g][1]
                    cols = NT * nh
                    r4 = raws[:, g % 2, :, 0:nh * HD].rearrange("p b (h c) -> p b h c", h=nh)
                    sq = head_sq[:, 0:cols * HD].rearrange("p (b h c) -> p b h c", b=NT, h=nh)
                    if g > 0:
                        dve.wait_ge(tp_ready, g)
                    link.then(dve.tensor_tensor(sq, r4, r4, ALU.mult))
                    link.then(dve.tensor_reduce(st[:, 0, 0:cols], head_sq[:, 0:cols * HD].rearrange("p (n c) -> p n c", c=HD),
                                                AX.X, ALU.add))
                    inv_root(g + 1, cols, HD)
                    inv = st[:, 3, 0:cols].rearrange("p (b h) -> p b h", b=NT)
                    for b in range(NT):
                        rb = r4[:, b, :, :]
                        link(dve.tensor_tensor(rb, rb, inv[:, b, :].unsqueeze(2).to_broadcast([P, nh, HD]), ALU.mult))
                    link.upto(link.count)
                    for b in range(NT):
                        rb = r4[:, b, :, :]
                        link(dve.tensor_tensor(rb, rb, qk_gain[:, g // 2, :].unsqueeze(1).to_broadcast([P, nh, HD]), ALU.mult))
                    link.upto(link.count)
                    rotate(r4[:, :, :, 0:ROPE_Q], r4[:, :, :, ROPE_Q:2 * ROPE_Q], cos_q, sin_q, [P, NT, nh, ROPE_Q])
                else:
                    nh = IH if g == 3 else 2
                    dve.wait_ge(tp_ready, g)
                    r4 = raws[:, g % 2, :, 0:nh * ID].rearrange("p b (h c) -> p b h c", h=nh)
                    rotate(r4[:, :, :, 0:ROPE_I], r4[:, :, :, ROPE_I:2 * ROPE_I], cos_i, sin_i, [P, NT, nh, ROPE_I])

            for b in range(1, NT):
                for h in range(IH):
                    n = IH * (b - 1) + h
                    dve.wait_ge(id_relu, n + 1)
                    r = relus[:, n % 2, 0:mask_cols[b]]
                    if h == 0:
                        dve.tensor_scalar(masks[b], r, wi[:, b, 0:1], None, ALU.mult).then_inc(id_used, 1)
                    else:
                        dve.wait_ge(id_used, n)
                        dve.scalar_tensor_tensor(masks[b], r, wi[:, b, h:h + 1], masks[b], ALU.mult, ALU.add).then_inc(id_used, 1)
                dve.wait_ge(id_used, IH * b)
                link(dve.tensor_tensor(masks[b][:, b * P:], masks[b][:, b * P:], tri, ALU.add))
            link.upto(link.count)
            for b in range(1, NT):
                for _ in range(TOPK_KEYS // 8):
                    link.then(dve.max(mx8, masks[b]))
                    link.then(dve.match_replace(masks[b], mx8, masks[b], TAKEN))
                link.then(dve.tensor_scalar(masks[b], masks[b], TAKEN / 2, MASKED, ALU.is_gt, ALU.mult))

            dve.nop(nofuse=True).then_inc(cv_done, 4)
            link.then(dve.memset(u_pad[:, :, 0:CONV_K - 1], 0.0))
            PER = 4 * 6
            with dve.Fori(0, KC // 4) as mm:
                m = mm * 4
                link.enter(mm, PER)
                for s in range(4):
                    dve.wait_ge(cp_out, m * 5 + (4 + 5 * s + 4))
                    w = taps[:, bass.ds(m + s, 1), :]
                    u = u_pad[:, s % 2, :]
                    link.then(dve.tensor_tensor(u[:, CONV_K - 1:], chan_sets[:, s, 0, :], chan_sets[:, s, 1, :], ALU.mult))
                    link.then(dve.tensor_scalar(conv, u[:, 0:SEQ], w[:, 0, 0:1], None, ALU.mult))
                    for j in range(1, CONV_K):
                        link.then(dve.scalar_tensor_tensor(conv, u[:, j:j + SEQ], w[:, 0, j:j + 1], conv, ALU.mult, ALU.add))
                    link.then(dve.tensor_tensor(conv, conv, chan_sets[:, s, 2, :], ALU.mult))
                    link.then(dve.tensor_tensor(mixed[:, bass.ds(m + s, 1), :].rearrange("p a t -> p (a t)"), conv,
                                                chan_sets[:, s, 3, :], ALU.mult))
                    dve.nop(nofuse=True).then_inc(cv_done, 1)
                link.leave(KC // 4)

            for step in range(UNITS + 4):
                if step < UNITS:
                    b, h = divmod(step, HEADS)
                    dve.wait_ge(s_done, step + 1)
                    if step >= 2:
                        dve.wait_ge(p_turned, step - 1)
                    cols = mask_cols[b]
                    bias = tri if b == 0 else masks[b]
                    link.then(dve.tensor_tensor_reduce(out=probs[:, step % 2, 0:cols], in0=banks[:, step % 2, 0:cols], in1=bias,
                                                       scale=1.0, scalar=TAKEN, op0=ALU.add, op1=ALU.max,
                                                       accum_out=sm[:, step % 2, 0:1]))
                    dve.tensor_scalar(sm[:, step % 2, 1:2], sm[:, step % 2, 0:1], -ATTN_SCALE, None, ALU.mult).then_inc(s_max, 1)
                n = step - 1
                if 0 <= n < UNITS:
                    b, h = divmod(n, HEADS)
                    dve.wait_ge(s_exp, n + 1)
                    link.then(dve.reciprocal(sm[:, n % 2, 3:4], sm[:, n % 2, 2:3]))
                    dve.tensor_scalar(probs[:, n % 2, 0:mask_cols[b]], probs[:, n % 2, 0:mask_cols[b]], sm[:, n % 2, 3:4],
                                      None, ALU.mult).then_inc(s_prob, 1)
                n = step - 4
                if n >= 0:
                    b, h = divmod(n, HEADS)
                    dve.wait_ge(o_done, n + 1)
                    if n == 0:
                        dve.wait_ge(cp_out, 4 + 5 * KC)
                    tb = slice(b * P, (b + 1) * P)
                    link.then(dve.tensor_tensor(gate_b[:, h, tb], banks[:, 2 + n % 2, 0:P], gate_b[:, h, tb], ALU.mult))
                    dve.tensor_tensor(mixed[:, h, tb], mixed[:, h, tb], gate_b[:, h, tb], ALU.add).then_inc(o_used, 1)

            for b in range(NT):
                for s in range(2):
                    dve.wait_ge(y_done, 2 * b + s + 1)
                    half = resid[:, b, s * 512:(s + 1) * 512]
                    dve.tensor_tensor(half, banks[:, 6 + s, :], half, ALU.add).then_inc(y_out, 1)
            dve.wait_ge(n_sq, 2 * NT)
            dve.wait_ge(o_used, UNITS)
            inv_root(4, NT, D)
            norm_out(2 * NT, g2)

            dve.nop(nofuse=True).then_inc(k_out, 2)
            score4 = scores[:, 0:ITERS * 2 * NKEY].rearrange("p (b j n) -> p b j n", b=NT, j=2 * PH)
            with dve.Fori(0, 2 * PH // 4) as jj:
                j = jj * 4
                for s in range(4):
                    dve.wait_ge(k_done, j + (s + 1))
                    dve.nop(nofuse=True)
                    dve.tensor_copy(score4[:, :, bass.ds(j + s, 1), :].rearrange("p b a n -> p b (a n)"),
                                    banks[:, 2 + s % 2, :].rearrange("p (b n) -> p b n", b=NT)).then_inc(k_out, 1)

            def route_keys():
                for a in range(2):
                    ta = link(dve.max(topv[:, a, 0:8], sc[:, a, :]))
                link.upto(ta)
                for a in range(2):
                    link(dve.max_index(topi[:, a, 0:8], topv[:, a, 0:8], sc[:, a, :]))
                    ta = link(dve.match_replace(sc_cut[:, a, :], topv[:, a, 0:8], sc[:, a, :], TAKEN))
                link.upto(ta)
                for a in range(2):
                    ta = link(dve.max(topv[:, a, 8:16], sc_cut[:, a, :]))
                link.upto(ta)
                for a in range(2):
                    ta = link(dve.max_index(topi[:, a, 8:16], topv[:, a, 8:16], sc_cut[:, a, :]))
                link.upto(ta)
                link(dve.tensor_copy(topif, topi))

            def route_pairs():
                link.then(dve.tensor_tensor(cand.rearrange("p (k n) -> p k n", k=PTOP),
                                            topv[:, 0, :].unsqueeze(2).to_broadcast([P, PTOP, PTOP]),
                                            topv[:, 1, :].unsqueeze(1).to_broadcast([P, PTOP, PTOP]), ALU.add))
                link.then(dve.max(best[:, 0:8], cand))
                link(dve.max_index(pos[:, 0:8], best[:, 0:8], cand))
                link.then(dve.match_replace(cand_cut, best[:, 0:8], cand, TAKEN))
                link.then(dve.max(best[:, 8:16], cand_cut))
                link(dve.max_index(pos[:, 8:16], best[:, 8:16], cand_cut))
                dve.tensor_scalar(gstat[:, 0:1], best[:, 0:1], -1.0, None, ALU.mult).then_inc(r_max, 1)
                link.upto(link.count)

            def route_experts(s, exps):
                link(dve.tensor_scalar(posij[:, 0, :], pos, 4, None, ALU.logical_shift_right))
                link.then(dve.tensor_scalar(posij[:, 1, :], pos, 15, None, ALU.bitwise_and))
                link.then(dve.tensor_copy(posf, posij))
                for a in range(2):
                    link(dve.tensor_tensor(onehot[:, a, :, :], posf[:, a, :].unsqueeze(2).to_broadcast([P, PTOP, PTOP]),
                                           iota.unsqueeze(1).to_broadcast([P, PTOP, PTOP]), ALU.is_equal))
                link.upto(link.count)
                for a in range(2):
                    link(dve.tensor_tensor(onehot[:, a, :, :], onehot[:, a, :, :],
                                           topif[:, a, :].unsqueeze(1).to_broadcast([P, PTOP, PTOP]), ALU.mult))
                link.upto(link.count)
                link.then(dve.tensor_reduce(chosen, onehot, AX.X, ALU.add))
                dve.wait_ge(r_exp, exps)
                link(dve.reciprocal(gstat[:, 2:3], gstat[:, 1:2]))
                link.then(dve.scalar_tensor_tensor(eidx[:, s, :], chosen[:, 0, :], float(NKEY), chosen[:, 1, :], ALU.mult, ALU.add))
                dve.tensor_scalar(gprob[:, s, :], gprob[:, s, :], gstat[:, 2:3], None, ALU.mult).then_inc(r_done, 1)

            dve.nop(nofuse=True).then_inc(acc_free, 2)
            dve.wait_ge(r_in, 1)
            route_keys()
            route_pairs()
            route_experts(0, 1)
            link.upto(link.count)
            ROUTE_LINKS = 11 + 6 + 10
            with dve.Fori(0, ITERS // 2) as ii:
                i = ii * 2
                link.enter(ii, 2 * ROUTE_LINKS)
                for s in range(2):
                    dve.wait_ge(cur_in, i + (s + 1))
                    for q in range(4):
                        for k in range(4 * q, 4 * q + 4):
                            n = PTOP * s + k
                            dve.wait_ge(row_in[k % RING], i * 32 + 16 * (2 * s + k // RING + 1))
                            if k % 4 >= 2:
                                dve.wait_ge(dot_done, i * PTOP + (n - 1))
                            dve.tensor_tensor_reduce(out=dotjunk[:, k % 2, :], in0=slots[:, k % RING, 0:D], in1=xcur[:, s, :],
                                                     scale=1.0, scalar=0.0, op0=ALU.mult, op1=ALU.add,
                                                     accum_out=dots[:, k:k + 1]).then_inc(dot_done, 1)
                        dve.wait_ge(gel_done, i * 4 + (4 * s + q + 1))
                        if q == 0:
                            dve.wait_ge(r_done, i + (s + 1))
                        for k in range(4 * q, 4 * q + 4):
                            n = PTOP * s + k
                            dve.wait_ge(row_free, i * PTOP + (n + 1 + RING - DIAGS))
                            dve.tensor_scalar(diag[:, k % DIAGS, :], ident, gel[:, k:k + 1], gprob[:, s, k:k + 1],
                                              ALU.mult, ALU.mult).then_inc(diag_done, 1)
                        if q == 0:
                            dve.wait_ge(r_in, i + (s + 2))
                            dve.nop(nofuse=True)
                            route_keys()
                        if q == 1:
                            link.upto(link.count)
                            route_pairs()
                            route_experts(1 - s, i + (s + 2))
                    dve.wait_ge(row_free, i * PTOP + (PTOP * (s + 1) + RING))
                    blk = resid[:, bass.ds(i // PH, 1), :].rearrange("p a (h c) -> p (a h) c", h=2)
                    dve.wait_ge(acc_free, i + (s + 2))
                    dve.tensor_tensor(blk, banks[:, 4 + 2 * s:6 + 2 * s, :], blk, ALU.add).then_inc(acc_free, 1)
                link.leave(ITERS // 2)


def kernel(x, norm1_g, w_in, conv_w, q_norm_g, k_norm_g, w_o, norm2_g, peer_wq, peer_k1, peer_k2, peer_u, peer_v):
    import numpy as np
    import concourse.bacc as bacc
    from concourse.bass_utils import run_bass_kernel_spmd

    a = {k: np.asarray(v) for k, v in dict(
        x=x, norm1_g=norm1_g, w_in=w_in, conv_w=conv_w, q_norm_g=q_norm_g, k_norm_g=k_norm_g, w_o=w_o, norm2_g=norm2_g,
        peer_wq=peer_wq, peer_k1=peer_k1, peer_k2=peer_k2, peer_u=peer_u, peer_v=peer_v).items()}

    def chunks(w, cols):
        n = w.shape[1] // cols
        return np.ascontiguousarray(w.reshape(KC, P, n, cols).transpose(2, 1, 0, 3)).reshape(n, P, KC * cols)

    w = a["w_in"]
    tok = w[:, 3 * D:]
    n_tok = D + 2 * KVH * HD + IH * ID
    small = ID + IH
    ga0 = 3 * D + n_tok + small
    sel = [w[:, D:2 * D], w[:, 2 * D:3 * D], w[:, 0:D], w[:, ga0:ga0 + D], w[:, ga0 + D:ga0 + 2 * D]]
    w_chan = np.ascontiguousarray(np.stack([chunks(s, P) for s in sel], axis=2)).reshape(KC, P, 5 * KC * P)

    t = np.arange(SEQ, dtype=np.float32)[:, None]

    def table(fn, half):
        inv = (np.float32(500000.0) ** (-np.arange(half, dtype=np.float32) / np.float32(half))).astype(np.float32)
        v = fn((t * inv[None, :]).astype(np.float32).astype(np.float64)).astype(np.float32)
        return v.reshape(NT, P, half).transpose(1, 0, 2).reshape(P, NT * half)

    lower = np.where(np.arange(P)[None, :] <= np.arange(P)[:, None], 0.0, MASKED).astype(np.float32)
    consts = np.concatenate([np.eye(P, dtype=np.float32), lower, np.tile(np.arange(16, dtype=np.float32), (P, 1)),
                             table(np.cos, ROPE_Q), table(np.sin, ROPE_Q), table(np.cos, ROPE_I), table(np.sin, ROPE_I)], axis=1)
    params = np.concatenate([a["norm1_g"].reshape(KC, P).T, a["norm2_g"].reshape(KC, P).T,
                             a["conv_w"].reshape(CONV_K, KC, P).transpose(2, 1, 0).reshape(P, KC * CONV_K)], axis=1)
    arrays = {
        "x": a["x"].reshape(SEQ, D),
        "w_tok": chunks(tok[:, 0:n_tok], 512),
        "w_small": chunks(tok[:, n_tok:n_tok + small], small)[0],
        "w_chan": w_chan,
        "w_out": chunks(a["w_o"], 512),
        "w_q": chunks(a["peer_wq"], P),
        "keys_t": np.ascontiguousarray(np.stack([a["peer_k1"], a["peer_k2"]], axis=1).transpose(0, 1, 3, 2)).reshape(2 * PH, P, NKEY),
        "uv": np.concatenate([a["peer_u"], a["peer_v"]], axis=1),
        "consts": consts,
        "params": params,
        "rows": np.concatenate([a["norm2_g"], a["q_norm_g"], a["k_norm_g"]]),
    }
    arrays = {k: np.ascontiguousarray(v) for k, v in arrays.items()}
    nc = bacc.Bacc("TRN2", target_bir_lowering=False, num_devices=1)
    args = [nc.dram_tensor("in_" + k, v.shape, F32, kind="ExternalInput").ap() for k, v in arrays.items()]
    out = nc.dram_tensor("out_h", (SEQ, D), F32, kind="ExternalOutput").ap()
    build(nc, *args, out)
    r = run_bass_kernel_spmd(nc, [{"in_" + k: v for k, v in arrays.items()}], core_ids=[0])
    return r.results[0]["out_h"].reshape(1, SEQ, D)
```

```python
from contextlib import ExitStack

import concourse.bass as bass
from concourse import mybir

ALU = mybir.AluOpType
ACT = mybir.ActivationFunctionType
AX = mybir.AxisListType
F32 = mybir.dt.float32
FR = mybir.dt.float32r
U32 = mybir.dt.uint32

P = 128
SEQ, D = 512, 1024
NT = SEQ // P
KC = D // P
HEADS, HD, KVH = 8, 128, 2
GROUP = HEADS // KVH
IH, ID = 8, 64
TOPK_KEYS = min(256, SEQ // 4)
PH, NKEY, PTOP = 8, 128, 16
CONV_K = 3
EPS = 1e-6
ATTN_SCALE = HD ** -0.5
IDX_SCALE = ID ** -0.5
IDX_W_SCALE = IH ** -0.5
ROPE_Q, ROPE_I = HD // 4 // 2, ID // 4 // 2
MASKED = -1.0e30
TAKEN = -3.0e38
RING = 8
DIAGS = 4
UNITS = NT * HEADS
ITERS = NT * PH
CONST_COLS = 128 + 128 + 16 + 2 * NT * ROPE_Q + 2 * NT * ROPE_I
WSLOTS = 4
UNIT = KC * P
TOK_KINDS = ("qi", "ki", "kv", "q0", "q1")
TOK_UNITS = (4, 1, 4, 4, 4)
TOK_START = (0, 4, 5, 9, 13, 17)
TURNS = (4, 1, 2, 4, 4)
TURN0 = (0, 4, 5, 7, 11, 15)
U_CHAN = TOK_START[-1]
U_OUT = U_CHAN + 5 * KC
U_QUERY = U_OUT + 2 * D // 512 * 2
Q_GROUPS = 2 * PH * P // 512
U_OUT2 = U_QUERY + 4 * Q_GROUPS
U_QUERY2 = U_OUT2 + 8
SRC_QUERY2 = U_QUERY + 4 * Q_GROUPS
G_ATT = 0
G_OUT = 16
OUT_SPLITS = {G_OUT - 3: (0, 1), G_OUT - 1: (2, 3), G_OUT + 2: (4, 5), G_OUT + 3: (6, 7)}
G_ADD = G_OUT + 3
G_NORM = G_OUT + 5
G_GAIN = G_NORM + 2
I_QUERY = 6
PARAM_COLS = KC + KC + KC * CONV_K


class Link:

    def __init__(self, eng, sem):
        self.eng, self.sem, self.count, self.var, self.per = eng, sem, 0, None, 0

    def __call__(self, ins):
        ins.then_inc(self.sem, 1)
        self.count += 1
        return self.count

    def upto(self, count):
        if self.var is None:
            self.eng.wait_ge(self.sem, count)
        else:
            self.eng.wait_ge(self.sem, self.var * self.per + count)
            self.eng.nop(nofuse=True)

    def then(self, ins):
        self.upto(self(ins))

    def enter(self, var, per):
        self.var, self.per, self.start = var, per, self.count

    def leave(self, trips):
        assert self.count - self.start == self.per, (self.count - self.start, self.per)
        self.count, self.var = self.start + trips * self.per, None


def build(nc, x, w_units, keys_t, uv, consts, params, rows, out):
    with ExitStack() as ctx:
        def sb(name, cols, dt=F32):
            return ctx.enter_context(nc.sbuf_tensor(name, [P, cols], dt))

        def sem(name):
            return ctx.enter_context(nc.semaphore(name))

        banks = ctx.enter_context(nc.psum_tensor("banks", [P, 8, 512], F32))
        regions = dict(ring=RING * 2 * D, xreg=KC * SEQ, resid=NT * D, qreg=HEADS * SEQ, mreg=KC * SEQ, big=(ITERS + 1) * 2 * NKEY)
        arena = sb("arena", sum(regions.values()))[:]
        arena_start = nc.sbuf_base - 4 * sum(regions.values())
        at, region = 0, {}
        for name, cols in regions.items():
            region[name] = (at, cols)
            at += cols

        def part(name):
            return arena[:, region[name][0]:region[name][0] + region[name][1]]

        def rounded(name, where, col, cols):
            return nc.alloc_sbuf_tensor_at(name, [P, cols], FR, offset=arena_start + 4 * (region[where][0] + col), align_bytes=32)[:]

        resid = part("resid").rearrange("p (b d) -> p b d", b=NT)
        tokmaj = sb("tokmaj", NT * D)[:]
        xn_tok = tokmaj.rearrange("p (b d) -> p b d", b=NT)
        gate_b = tokmaj.rearrange("p (m t) -> p m t", m=KC)
        x_hi = rounded("x_hi", "xreg", 0, KC * SEQ).rearrange("p (k t) -> p k t", k=KC)
        xn_full = part("resid").rearrange("p (k t) -> p k t", k=KC)
        xn_lo = rounded("xn_lo", "resid", 0, KC * SEQ).rearrange("p (k t) -> p k t", k=KC)
        hn_full = part("qreg").rearrange("p (k t) -> p k t", k=KC)
        hn_lo = rounded("hn_lo", "qreg", 0, KC * SEQ).rearrange("p (k t) -> p k t", k=KC)
        xn0 = sb("xn0", D)[:]
        big = part("big")
        scores = big
        chan_sets = big[:, 0:4 * 4 * SEQ].rearrange("p (s q t) -> p s q t", s=4, q=4)
        square = big[:, 0:D]
        square2 = part("qreg")[:, 0:D]
        ring = part("ring")
        slots = ring.rearrange("p (r e) -> p r e", r=RING)
        w_full = ring[:, 0:WSLOTS * UNIT].rearrange("p (s e) -> p s e", s=WSLOTS)
        w_lo = rounded("w_lo", "ring", 0, WSLOTS * UNIT).rearrange("p (s e) -> p s e", s=WSLOTS)
        w_hi = rounded("w_hi", "ring", WSLOTS * UNIT, WSLOTS * UNIT).rearrange("p (s e) -> p s e", s=WSLOTS)
        rest = 2 * WSLOTS * UNIT
        raws = ring[:, rest:rest + 2 * NT * 512].rearrange("p (s b c) -> p s b c", s=2, b=NT)
        tail = ring[:, rest + 2 * NT * 512:]
        relus = tail[:, 0:2 * SEQ].rearrange("p (s t) -> p s t", s=2)
        SIDE0 = PH * 2 * NKEY
        probs_first = tail[:, 2 * SEQ:4 * SEQ].rearrange("p (s t) -> p s t", s=2)
        probs_side = big[:, SIDE0:SIDE0 + 4 * SEQ].rearrange("p (s t) -> p s t", s=4)
        probsT_side = big[:, SIDE0 + 4 * SEQ:SIDE0 + 6 * SEQ].rearrange("p (s t) -> p s t", s=2)
        junk_early = big[:, SIDE0 + 8 * SEQ:SIDE0 + 8 * SEQ + 2 * D].rearrange("p (s d) -> p s d", s=2)
        g2row0 = ring[:, rest + NT * 512:rest + NT * 512 + D]
        key0 = ring[:, rest + NT * 512 + D:rest + NT * 512 + D + 2 * PH * NKEY].rearrange("p (j n) -> p j n", n=NKEY)
        free = rest + 2 * NT * 512 + 4 * SEQ
        qtok = raws[:, 0, 0:2, :]
        q2T0 = raws[:, 0, 2:4, :]
        kiT_low = ring[:, free:free + SEQ]
        hn0 = ring[:, free:free + D].rearrange("p (k t) -> p k t", k=KC)

        def xn_block(b):
            return xn_full[:, :, b * P:(b + 1) * P]

        def hn_block(b):
            return hn0 if b == 0 else hn_full[:, :, b * P:(b + 1) * P]

        def splits(u):
            return u + 1 - (U_OUT2 - U_QUERY if u >= U_OUT2 else 0)

        def unit_slot(name, where, col):
            full = part(where)[:, col:col + UNIT]
            return full, (rounded(name + "_hi", where, col + UNIT, UNIT), rounded(name + "_lo", where, col, UNIT))

        out_slots = [unit_slot(f"wo{s}", ("qreg", "big")[s // 2], SIDE0 * (s // 2) + 2 * UNIT * (s % 2)) for s in range(4)]
        query_slots = [unit_slot(f"wq{s}", "mreg", 2 * UNIT * s) for s in range(2)]

        def slot_of(u):
            if u < U_OUT2:
                s = u % WSLOTS
                return w_full[:, s, :], (w_hi[:, s, :], w_lo[:, s, :])
            return out_slots[(u - U_OUT2) % 4] if u < U_QUERY2 else query_slots[(u - U_QUERY2) % 2]

        UP = SEQ + CONV_K - 1
        u_pad = raws[:, 1, :, :].rearrange("p b c -> p (b c)")[:, 0:2 * UP].rearrange("p (s t) -> p s t", s=2)
        conv = raws[:, 1, :, :].rearrange("p b c -> p (b c)")[:, 2 * UP:2 * UP + SEQ]
        qT = part("qreg").rearrange("p (h t) -> p h t", h=HEADS)
        kreg = sb("kreg", KVH * SEQ)[:]
        kT = kreg.rearrange("p (h t) -> p h t", h=KVH)
        g2row = kreg
        SB = SEQ - P
        q2T = kreg[:, 0:2 * SB].rearrange("p (s t) -> p s t", s=2)
        vreg = sb("vreg", NT * KVH * HD)[:]
        v_tok = vreg.rearrange("p (b c) -> p b c", b=NT)
        key_sb = vreg[:, 0:4 * NKEY].rearrange("p (s e) -> p s e", s=2)
        ireg = sb("ireg", 4 * SEQ)[:]
        qiT = ireg.rearrange("p (h t) -> p h t", h=4)
        probsT_first = ireg[:, 0:2 * SEQ].rearrange("p (s t) -> p s t", s=2)
        sc = ireg[:, 0:256].rearrange("p (a n) -> p a n", a=2)
        sc_cut = ireg[:, 256:512].rearrange("p (a n) -> p a n", a=2)
        cand = ireg[:, 512:768]
        cand_cut = ireg[:, 768:1024]
        onehot = ireg[:, 1024:1536].rearrange("p (a k n) -> p a k n", a=2, k=PTOP)
        diag = ireg[:, 1536:2048].rearrange("p (s n) -> p s n", s=DIAGS)
        kiT = sb("kiT", SEQ)[:]
        mreg = part("mreg")
        mixed = mreg.rearrange("p (m t) -> p m t", m=KC)
        mixed_lo = rounded("mixed_lo", "mreg", 0, KC * SEQ).rearrange("p (m t) -> p m t", m=KC)
        head_sq = mreg[:, 0:NT * 512]
        turn = mreg[:, NT * 512:NT * 512 + 4 * NT * 4 * ROPE_Q].rearrange("p (q n) -> p q n", q=4)
        junk_late = mreg[:, 0:2 * D].rearrange("p (s d) -> p s d", s=2)
        mask_cols = [P * (b + 1) for b in range(NT)]
        mask_at = [sum(mask_cols[1:b]) for b in range(NT)]
        maskreg = sb("maskreg", sum(mask_cols[1:]))[:]
        masks = [maskreg[:, mask_at[b]:mask_at[b] + mask_cols[b]] for b in range(NT)]

        def dotjunk(i, k):
            if i < G_OUT // 4:
                return junk_early[:, k % 2, :]
            if i < I_QUERY + PH:
                return (maskreg[:, 0:D], xn_tok[:, 0, :])[k % 2]
            return junk_late[:, k % 2, :]
        cst = sb("cst", CONST_COLS)[:]
        ident, tri, iota = cst[:, 0:128], cst[:, 128:256], cst[:, 256:272]
        at = 272
        tables = []
        for half in (ROPE_Q, ROPE_Q, ROPE_I, ROPE_I):
            tables.append(cst[:, at:at + NT * half].rearrange("p (b r) -> p b r", b=NT))
            at += NT * half
        cos_q, sin_q, cos_i, sin_i = tables
        par = sb("par", PARAM_COLS)[:]
        g1, g2 = par[:, 0:KC], par[:, KC:2 * KC]
        taps = par[:, 2 * KC:].rearrange("p (m j) -> p m j", j=CONV_K)
        qk_gain = sb("qk_gain", 2 * HD)[:].rearrange("p (a c) -> p a c", a=2)
        wi = sb("wi", NT * IH)[:].rearrange("p (b h) -> p b h", b=NT)
        st = sb("st", 5 * 16)[:].rearrange("p (a n) -> p a n", a=5)
        mx8 = sb("mx8", 8)[:]
        sm = sb("sm", 16)[:].rearrange("p (s a) -> p s a", s=4)
        topv = kiT[:, 0:2 * PTOP].rearrange("p (a k) -> p a k", a=2)
        topi = sb("topi", 2 * PTOP, U32)[:].rearrange("p (a k) -> p a k", a=2)
        topif = kiT[:, 2 * PTOP:4 * PTOP].rearrange("p (a k) -> p a k", a=2)
        best = kiT[:, 12 * PTOP:13 * PTOP]
        pos = sb("pos", PTOP, U32)[:]
        posij = sb("posij", 2 * PTOP, U32)[:].rearrange("p (a k) -> p a k", a=2)
        posf = kiT[:, 4 * PTOP:6 * PTOP].rearrange("p (a k) -> p a k", a=2)
        chosen = kiT[:, 6 * PTOP:8 * PTOP].rearrange("p (a k) -> p a k", a=2)
        eidx = sb("eidx", 2 * PTOP, U32)[:].rearrange("p (s k) -> p s k", s=2)
        gprob = kiT[:, 8 * PTOP:10 * PTOP].rearrange("p (s k) -> p s k", s=2)
        gstat = sb("gstat", 3)[:]
        dots = kiT[:, 10 * PTOP:11 * PTOP]
        gel = kiT[:, 11 * PTOP:12 * PTOP]

        const_in = sem("const_in")
        x_in = [sem(f"x_in{b}") for b in range(NT)]
        x_again = sem("x_again")
        w_in = [sem(f"w_in{s}") for s in range(WSLOTS)]
        g2row_in = sem("g2row_in")
        key_in = sem("key_in")
        w_split = sem("w_split")
        w_ready = sem("w_ready")
        w_used = sem("w_used")
        x_split = sem("x_split")
        x_ready = sem("x_ready")
        wo2_in = [sem(f"wo2_in{s}") for s in range(4)]
        wq2_in = [sem(f"wq2_in{s}") for s in range(2)]
        g2again_in = sem("g2again_in")
        key2_in = [sem(f"key2_in{s}") for s in range(2)]
        m_split = sem("m_split")
        m_ready = sem("m_ready")
        n_sq = sem("n_sq")
        n_var = sem("n_var")
        n_root = sem("n_root")
        n_scaled = sem("n_scaled")
        n_turned = sem("n_turned")
        n_out = sem("n_out")
        tp_done = sem("tp_done")
        tp_out = sem("tp_out")
        tp_sq = sem("tp_sq")
        tp_ready = sem("tp_ready")
        tt_done = sem("tt_done")
        tt_out = sem("tt_out")
        id_done = sem("id_done")
        id_relu = sem("id_relu")
        id_used = sem("id_used")
        cp_out = sem("cp_out")
        cv_done = sem("cv_done")
        s_done = sem("s_done")
        s_max = sem("s_max")
        s_exp = sem("s_exp")
        s_prob = sem("s_prob")
        p_turned = sem("p_turned")
        p_out = sem("p_out")
        o_done = sem("o_done")
        o_used = sem("o_used")
        y_done = sem("y_done")
        y_out = sem("y_out")
        xn_ready = sem("xn_ready")
        q_out = sem("q_out")
        qt_done = sem("qt_done")
        qt_out = sem("qt_out")
        k_done = sem("k_done")
        k_out = sem("k_out")
        r_in = sem("r_in")
        r_max = sem("r_max")
        r_exp = sem("r_exp")
        r_done = sem("r_done")
        row_in = [sem(f"row_in{s}") for s in range(RING)]
        dot_done = sem("dot_done")
        gel_done = sem("gel_done")
        diag_done = sem("diag_done")
        row_free = sem("row_free")
        acc_free = sem("acc_free")
        out_in = sem("out_in")
        part_out = sem("part_out")
        pad_set = sem("pad_set")
        ch_dve = sem("ch_dve")

        block = ctx.enter_context(nc.Block())
        TOKG = len(TOK_KINDS)

        def for_all_iterations(eng, body, enter=None, leave=None):
            for i in range(PH):
                body(0, i)
            loops = [(PH, I_QUERY)] + [(b * PH, PH) for b in range(2, NT)]
            for first, count in loops:
                with eng.Fori(0, count // 2) as rr:
                    if enter:
                        enter(rr)
                    for s in range(2):
                        body(rr * 2, first + s)
                    if leave:
                        leave(count // 2)
                for i in range(first + count, (first // PH + 1) * PH):
                    body(0, i)

        @block.sync
        def _(sp):
            sp.dma_start(cst, consts).then_inc(const_in, 16)
            for b in range(NT):
                sp.dma_start(resid[:, b, :], x[b * P:(b + 1) * P, :]).then_inc(x_in[b], 16)
                if b == 0:
                    sp.dma_start(par, params).then_inc(const_in, 16)
                    sp.dma_start(qk_gain[:, 0, :], rows[D:D + HD].partition_broadcast(P)).then_inc(const_in, 16)
                    sp.dma_start(qk_gain[:, 1, :], rows[D + HD:D + 2 * HD].partition_broadcast(P)).then_inc(const_in, 16)

            def fetch(u0, u):
                unit = w_units[u] if isinstance(u0, int) else w_units[bass.ds(u0 + u, 1)].rearrange("a p e -> p (a e)")
                sp.dma_start(slot_of(u)[0], unit).then_inc(w_in[u % WSLOTS], 16)

            def fetch_next(first, count):
                with sp.Fori(0, count // WSLOTS) as tt:
                    t = tt * WSLOTS
                    for s in range(WSLOTS):
                        sp.wait_ge(w_used, t + (first + s - WSLOTS + 1))
                        fetch(t, first + s)
                for u in range(first + count - count % WSLOTS, first + count):
                    sp.wait_ge(w_used, u - WSLOTS + 1)
                    fetch(0, u)

            for u in range(WSLOTS):
                fetch(0, u)
            fetch_next(WSLOTS, U_OUT)
            sp.dma_start(resid, x.rearrange("(b p) d -> p b d", p=P)).then_inc(x_again, 16)
            sp.wait_ge(cv_done, 4 + KC)
            sp.dma_start(g2row0, rows[0:D].partition_broadcast(P)).then_inc(g2row_in, 16)
            sp.dma_start(key0, keys_t.rearrange("j p n -> p j n")).then_inc(key_in, 16)
            fetch_next(U_OUT + WSLOTS, 4 + 4 * Q_GROUPS)

            def fetch2(src, u):
                unit = w_units[src] if isinstance(src, int) else w_units[bass.ds(src, 1)].rearrange("a p e -> p (a e)")
                done = wo2_in[(u - U_OUT2) % 4] if u < U_QUERY2 else wq2_in[(u - U_QUERY2) % 2]
                sp.dma_start(slot_of(u)[0], unit).then_inc(done, 16)

            def fetch_keys(h, s):
                src = keys_t[bass.ds(2 * h, 2)].rearrange("j p n -> p j n")
                sp.dma_start(key_sb[:, s, :].rearrange("p (j n) -> p j n", j=2), src).then_inc(key2_in[s], 16)

            sp.wait_ge(s_done, UNITS)
            fetch2(U_OUT, U_OUT2)
            fetch2(U_OUT + 1, U_OUT2 + 1)
            sp.dma_start(g2row, rows[0:D].partition_broadcast(P)).then_inc(g2again_in, 16)
            sp.wait_ge(o_done, UNITS)
            for q in range(2, 8):
                if q >= 4:
                    sp.wait_ge(w_used, U_OUT2 + q - 3)
                fetch2(U_OUT + q, U_OUT2 + q)
            fetch_keys(0, 0)
            fetch_keys(1, 1)
            sp.wait_ge(w_used, U_QUERY2)
            fetch2(SRC_QUERY2, U_QUERY2)
            fetch2(SRC_QUERY2 + 1, U_QUERY2 + 1)

            def fetch_head(r, h):
                for a in range(2):
                    sp.wait_ge(w_used, 2 * r + (U_QUERY2 + 2 * h + a - 1))
                    fetch2(2 * r + (SRC_QUERY2 + 2 * h + a), U_QUERY2 + a)
                if not (isinstance(r, int) and r + h == PH - 1):
                    sp.wait_ge(k_done, 2 * r + (Q_GROUPS + 2 * h))
                    fetch_keys(r + (h + 1), (h + 1) % 2)

            with sp.Fori(0, PH // 2 - 1) as rr:
                fetch_head(rr * 2, 1)
                fetch_head(rr * 2, 2)
            fetch_head(0, PH - 1)
            sp.wait_ge(acc_free, 2 + ITERS)
            sp.dma_start(out.rearrange("(b p) d -> p b d", p=P), resid).then_inc(out_in, 16)
            sp.wait_ge(out_in, 16)

        @block.tensor
        def _(pe):
            def turn_block(src, scaled, m0, bank, waits=False):
                pe.wait_ge(n_scaled, scaled)
                for j in range(2):
                    if waits:
                        pe.wait_ge(n_out, m0 + j - 1)
                    for c in range(4):
                        ins = pe.transpose(banks[:, bank + j, c * P:(c + 1) * P],
                                           src[:, (4 * j + c) * P:(4 * j + c + 1) * P], ident)
                    ins.then_inc(n_turned, 1)

            def split_product(out, w, x, first, last):
                pe.matmul(out, w[0], x[0], start=first, stop=False)
                pe.matmul(out, w[0], x[1], start=False, stop=False)
                return pe.matmul(out, w[1], x[0], start=False, stop=last)

            def unit_parts(u, k):
                return [w.rearrange("p (k c) -> p k c", k=k) for w in slot_of(u)[1]]

            pe.nop(nofuse=True).then_inc(row_free, RING)
            pe.wait_ge(const_in, 64)
            for b in range(NT):
                turn_block(xn_tok[:, b, :], b + 1, 2 * b, 4, b > 0)

            def token_projection(g):
                units = TOK_UNITS[g]
                chunks_in = KC // units
                cols = 512 if units > 1 else ID + IH
                for q in range(units):
                    u = TOK_START[g] + q
                    pe.wait_ge(w_ready, u + 1)
                    wh, wl = unit_parts(u, chunks_in)
                    for b in range(NT):
                        n = NT * g + b
                        tb = slice(b * P, (b + 1) * P)
                        if g == 0 and q == 0:
                            pe.wait_ge(x_ready, 2 * b + 2)
                        if q == 0 and g >= 1:
                            pe.wait_ge(tp_out, n - 3)
                        for c in range(chunks_in):
                            k = chunks_in * q + c
                            ins = split_product(banks[:, b, 0:cols], (x_hi[:, k, tb], xn_lo[:, k, tb]),
                                                (wh[:, c, 0:cols], wl[:, c, 0:cols]), k == 0, k == KC - 1)
                        if b == NT - 1:
                            ins.then_inc(w_used, 1)
                        elif q == units - 1:
                            ins.then_inc(tp_done, 1)

            def token_turns(g):
                pe.wait_ge(tp_ready, g + 1)
                for j in range(TURNS[g]):
                    m = TURN0[g] + j
                    if m >= 2:
                        pe.wait_ge(tt_out, m - 1)
                    for b in range(NT):
                        ins = pe.transpose(banks[:, 4 + m % 2, b * P:(b + 1) * P],
                                           raws[:, g % 2, b, j * P:(j + 1) * P], ident)
                    ins.then_inc(tt_done, 1)

            for g in range(TOKG):
                token_projection(g)
                if g >= 1:
                    token_turns(g - 1)
            pe.wait_ge(tt_out, TURN0[2])
            pe.wait_ge(part_out, 2 * NT + 1)
            pe.wait_ge(pad_set, 3)
            for b in range(1, NT):
                for h in range(IH):
                    n = IH * (b - 1) + h
                    if n >= 2:
                        pe.wait_ge(id_relu, n - 1)
                    pe.matmul(banks[:, 6 + n % 2, 0:mask_cols[b]], qiT[:, h // 2, b * P:(b + 1) * P],
                              (kiT, kiT_low)[h % 2][:, 0:mask_cols[b]], start=True, stop=True).then_inc(id_done, 1)
            pe.wait_ge(tp_out, NT * TOKG)
            with pe.Fori(0, KC // 4) as mm:
                m = mm * 4
                for n in range(20):
                    pe.wait_ge(w_ready, m * 5 + (U_CHAN + n + 1))
                    pe.wait_ge(cp_out, m * 5 + (n + 1))
                    wh, wl = unit_parts(U_CHAN + n, KC)
                    for k in range(KC):
                        ins = split_product(banks[:, n % 4, :], (wh[:, k, :], wl[:, k, :]), (x_hi[:, k, :], xn_lo[:, k, :]),
                                            k == 0, k == KC - 1)
                    ins.then_inc(w_used, 1)
            def att_scores(n):
                b, h = divmod(n, HEADS)
                if n >= 2:
                    pe.wait_ge(s_max, n - 1)
                pe.matmul(banks[:, n % 2, 0:mask_cols[b]], qT[:, h, b * P:(b + 1) * P],
                          kT[:, h // GROUP, 0:mask_cols[b]], start=True, stop=True).then_inc(s_done, 1)

            def att_turn(n, probs, bank):
                pe.wait_ge(s_prob, n + 1)
                if n >= 2:
                    pe.wait_ge(p_out, n - 1)
                for c in range(n // HEADS + 1):
                    ins = pe.transpose(banks[:, bank, c * P:(c + 1) * P], probs[:, c * P:(c + 1) * P], ident)
                ins.then_inc(p_turned, 1)

            def att_values(n, probsT, acc, merged):
                b, h = divmod(n, HEADS)
                pe.wait_ge(p_out, n + 1)
                if merged > 0:
                    pe.wait_ge(o_used, merged)
                for c in range(b + 1):
                    ins = pe.matmul(acc, v_tok[:, c, h // GROUP * HD:(h // GROUP + 1) * HD],
                                    probsT[:, c * P:(c + 1) * P], start=(c == 0), stop=(c == b))
                ins.then_inc(o_done, 1)

            token_turns(TOKG - 1)
            pe.wait_ge(cp_out, 4 + 5 * KC)
            pe.wait_ge(tt_out, TURN0[-2])
            for step in range(HEADS + 3):
                if step == 2:
                    pe.wait_ge(tt_out, TURN0[-1])
                if step < HEADS:
                    att_scores(step)
                n = step - 2
                if 0 <= n < HEADS:
                    att_turn(n, probs_first[:, n % 2, :], 4 + n % 2)
                n = step - 3
                if n >= 0:
                    att_values(n, probsT_first[:, n % 2, :], banks[:, 2 + n % 2, 0:P], n - 1)

            def out_unit(u, q, blocks, bank):
                pe.wait_ge(w_ready, splits(u))
                wh, wl = unit_parts(u, 2)
                for n, b in enumerate(blocks):
                    tb = slice(b * P, (b + 1) * P)
                    for c in range(2):
                        k = 2 * q + c
                        ins = split_product(banks[:, bank[n], :], (x_hi[:, k, tb], mixed_lo[:, k, tb]),
                                            (wh[:, c, :], wl[:, c, :]), k == 0, k == KC - 1)
                ins.then_inc(w_used, 1)

            pe.wait_ge(m_ready, 1)
            for q in range(8):
                out_unit(U_OUT + q, q % 4, [0], [6 + q // 4])
            turn_block(xn0, NT + 1, 2 * NT, 4)
            pe.wait_ge(n_out, 2 * NT + 2)
            pe.wait_ge(key_in, 16)
            for g in range(Q_GROUPS + 2):
                if g < Q_GROUPS:
                    for q in range(4):
                        u = U_QUERY + 4 * g + q
                        pe.wait_ge(w_in[u % WSLOTS], 16 * (u // WSLOTS + 1))
                        if q == 0 and g >= 2:
                            pe.wait_ge(q_out, g - 1)
                        w = slot_of(u)[0].rearrange("p (k c) -> p k c", k=2)
                        for c in range(2):
                            k = 2 * q + c
                            ins = pe.matmul(banks[:, g % 2, :], hn0[:, k, :], w[:, c, :], start=(k == 0), stop=(k == KC - 1))
                        ins.then_inc(w_used, 1)
                n = g - 1
                if 0 <= n < Q_GROUPS:
                    pe.wait_ge(q_out, n + 1)
                    if n >= 2:
                        pe.wait_ge(qt_out, n - 1)
                    for c in range(4):
                        ins = pe.transpose(banks[:, 2 + n % 2, c * P:(c + 1) * P], qtok[:, n % 2, c * P:(c + 1) * P], ident)
                    ins.then_inc(qt_done, 1)
                n = g - 2
                if n >= 0:
                    pe.wait_ge(qt_out, n + 1)
                    if n >= 2:
                        pe.wait_ge(k_out, n - 1)
                    for c in range(4):
                        ins = pe.matmul(banks[:, 4 + n % 2, c * P:(c + 1) * P], q2T0[:, n % 2, c * P:(c + 1) * P],
                                        key0[:, 4 * n + c, :], start=True, stop=True)
                    ins.then_inc(k_done, 1)

            def side(g):
                ga = g - G_ATT
                for j in range(2):
                    n = HEADS + 2 * ga - 4 + j
                    if HEADS <= n < UNITS:
                        att_turn(n, probs_side[:, n % 4, :], 2 + j)
                    n = HEADS + 2 * ga + j
                    if n < UNITS:
                        att_scores(n)
                for j in range(2):
                    n = HEADS + 2 * ga - 6 + j
                    if HEADS <= n < UNITS:
                        att_values(n, probsT_side[:, j, :], banks[:, 6, j * P:(j + 1) * P], n - j)
                if G_OUT <= g < G_OUT + 4:
                    if g == G_OUT:
                        pe.wait_ge(m_ready, NT)
                        pe.wait_ge(o_used, UNITS)
                    for q in range(2 * (g - G_OUT), 2 * (g - G_OUT) + 2):
                        out_unit(U_OUT2 + q, q % 4, [1, 2, 3], ([0, 1, 2], [3, 6, 7])[q // 4])
                if g == G_NORM:
                    for b, bank in ((1, 0), (2, 2), (3, 6)):
                        turn_block(xn_tok[:, b, :], NT + 1 + b, 2 * NT + 2 * b, bank)

            def side_query(r, h, a):
                if isinstance(r, int) and h + a == 0:
                    pe.wait_ge(x_ready, 4 * NT - 2)
                pe.wait_ge(w_ready, 2 * r + splits(U_QUERY2 + 2 * h + a))
                pe.wait_ge(q_out, 2 * r + (Q_GROUPS + 2 * h + a - 1))
                wh, wl = unit_parts(U_QUERY2 + a, KC)
                for k in range(KC):
                    ins = split_product(banks[:, a, 0:SB], (wh[:, k, :], wl[:, k, :]), (x_hi[:, k, P:], hn_lo[:, k, P:]),
                                        k == 0, k == KC - 1)
                ins.then_inc(w_used, 1)

            def side_keyscore(r, h, a):
                if a == 0:
                    pe.wait_ge(key2_in[h % 2], 8 * r + 16 * (h // 2 + 1))
                pe.wait_ge(q_out, 2 * r + (Q_GROUPS + 2 * h + a + 1))
                pe.wait_ge(k_out, 2 * r + (Q_GROUPS + 2 * h + a - 1))
                for b in range(NT - 1):
                    ins = pe.matmul(banks[:, 2 + a, b * P:(b + 1) * P], q2T[:, a, b * P:(b + 1) * P],
                                    key_sb[:, h % 2, a * NKEY:(a + 1) * NKEY], start=True, stop=True)
                ins.then_inc(k_done, 1)

            def experts(r, i):
                late = i >= I_QUERY
                pair = i % 2 if late else 0
                pe.wait_ge(acc_free, r + (i + (1 if i > I_QUERY else 2)))
                for k in range(PTOP):
                    pe.wait_ge(diag_done, r * PTOP + (i * PTOP + k + 1))
                    for s in range(2):
                        ins = pe.matmul(banks[:, 4 + 2 * pair + s, :], diag[:, k % DIAGS, :],
                                        slots[:, k % RING, D + s * 512:D + (s + 1) * 512],
                                        start=(k == 0), stop=(k == PTOP - 1))
                    ins.then_inc(row_free, 1)
                    if k % 4 == 3:
                        q = k // 4
                        if i < I_QUERY:
                            side(4 * i + q)
                        elif i < I_QUERY + PH:
                            h = i - I_QUERY
                            if q in (1, 2):
                                side_keyscore(r, h, q - 1)
                            if q in (0, 1):
                                side_query(r, h, q)

            for_all_iterations(pe, experts)
        @block.scalar
        def _(act):
            def split_weights(r, u):
                act.wait_ge(w_in[u % WSLOTS], r + 16 * (u // WSLOTS + 1))
                if not isinstance(r, int):
                    act.nop(nofuse=True)
                full, (hi, lo) = slot_of(u)
                act.activation(hi, full, ACT.Copy).then_inc(w_split, 1)

            def split_norm(blocks, full):
                for b in blocks:
                    for j in range(2):
                        act.wait_ge(n_out, 2 * b + j + (1 if full is xn_block else 2 * NT + 1))
                        act.activation(x_hi[:, 4 * j:4 * j + 4, b * P:(b + 1) * P], full(b)[:, 4 * j:4 * j + 4, :],
                                       ACT.Copy).then_inc(x_split, 1)

            def squares(n, b, col, junk):
                if n >= 1:
                    act.wait_ge(n_sq, n)
                act.activation(junk, resid[:, b, :], ACT.Square, accum_out=st[:, 0, col:col + 1]).then_inc(n_sq, 1)

            def root(n, cols):
                act.wait_ge(n_var, n + 1)
                act.activation(st[:, 2, 0:cols], st[:, 1, 0:cols], ACT.Sqrt).then_inc(n_root, 1)

            for b in range(NT):
                act.wait_ge(x_in[b], 16)
                squares(b, b, b, square)
            root(0, NT)
            for u in range(WSLOTS):
                split_weights(0, u)
            split_norm(range(NT), xn_block)

            def copy_out(g):
                ahead = list(range(TOK_START[g] + WSLOTS, TOK_START[g + 1] + WSLOTS - 1))
                for u in ahead[0:1]:
                    split_weights(0, u)
                if g >= 3:
                    root(g - 2, (8, 16)[g - 3])
                for u in ahead[1:]:
                    split_weights(0, u)
                for b in range(NT):
                    n = NT * g + b
                    if b < NT - 1:
                        act.wait_ge(tp_done, (NT - 1) * g + b + 1)
                    else:
                        act.wait_ge(w_used, TOK_START[g + 1])
                    if b == 0 and g >= 2:
                        act.wait_ge(tt_done, TURN0[g - 2] + TURNS[g - 2])
                    if g == 0 and b == 0:
                        act.wait_ge(n_sq, NT)
                    if TOK_KINDS[g] == "kv":
                        act.activation(raws[:, g % 2, b, 0:256], banks[:, b, 0:256], ACT.Copy).then_inc(part_out, 1)
                        act.activation(v_tok[:, b, :], banks[:, b, 256:512], ACT.Copy).then_inc(tp_out, 1)
                    elif TOK_KINDS[g] == "ki":
                        act.activation(raws[:, g % 2, b, 0:64], banks[:, b, 0:64], ACT.Copy).then_inc(part_out, 1)
                        act.activation(raws[:, g % 2, b, 64:128], banks[:, b, 0:64], ACT.Copy).then_inc(part_out, 1)
                        act.activation(wi[:, b, :], banks[:, b, 64:72], ACT.Copy, scale=IDX_W_SCALE).then_inc(tp_out, 1)
                    else:
                        act.activation(raws[:, g % 2, b, :], banks[:, b, :], ACT.Copy).then_inc(tp_out, 1)

            def turns_out(g):
                for j in range(TURNS[g]):
                    m = TURN0[g] + j
                    act.wait_ge(tt_done, m + 1)
                    if TOK_KINDS[g] == "ki":
                        act.activation(kiT[0:64], banks[0:64, 4 + m % 2, :], ACT.Copy).then_inc(part_out, 1)
                        act.activation(kiT_low[64:P], banks[64:P, 4 + m % 2, :], ACT.Copy).then_inc(tt_out, 1)
                        continue
                    dst = {"q0": qT[:, j, :], "q1": qT[:, 4 + j, :], "kv": kT[:, j % 2, :], "qi": qiT[:, j, :]}[TOK_KINDS[g]]
                    act.activation(dst, banks[:, 4 + m % 2, :], ACT.Copy).then_inc(tt_out, 1)

            act.nop(nofuse=True).then_inc(cp_out, 4)
            for g in range(TOKG):
                copy_out(g)
                if g >= 1:
                    turns_out(g - 1)
                split_weights(0, TOK_START[g + 1] + WSLOTS - 1)
            for b in range(1, NT):
                for h in range(IH):
                    n = IH * (b - 1) + h
                    act.wait_ge(id_done, n + 1)
                    if n >= 2:
                        act.wait_ge(id_used, n - 1)
                    act.activation(relus[:, n % 2, 0:mask_cols[b]], banks[:, 6 + n % 2, 0:mask_cols[b]],
                                   ACT.Relu, scale=IDX_SCALE).then_inc(id_relu, 1)
            root(TOKG - 2, 16)
            act.wait_ge(n_scaled, NT)
            act.wait_ge(n_turned, 2 * NT)
            with act.Fori(0, KC // 4) as mm:
                m = mm * 4
                for s in range(4):
                    for q in range(5):
                        n = 5 * s + q
                        act.wait_ge(w_used, m * 5 + (U_CHAN + n + 1))
                        if q == 0:
                            act.wait_ge(cv_done, m + (s + 1))
                        act.nop(nofuse=True)
                        dst = chan_sets[:, s, q, :] if q < 4 else gate_b[:, bass.ds(m + s, 1), :].rearrange("p a t -> p (a t)")
                        act.activation(dst, banks[:, n % 4, :], ACT.Copy if q < 3 else ACT.Sigmoid).then_inc(cp_out, 1)
                        split_weights(m * 20, U_CHAN + n + WSLOTS)

            def split_mixed(b):
                act.wait_ge(o_used, HEADS * (b + 1))
                tb = slice(b * P, (b + 1) * P)
                act.activation(x_hi[:, :, tb], mixed[:, :, tb], ACT.Copy).then_inc(m_split, 1)

            def att_exp(n, probs):
                act.wait_ge(s_max, n + 1)
                act.activation(probs[:, 0:mask_cols[n // HEADS]], probs[:, 0:mask_cols[n // HEADS]], ACT.Exp,
                               bias=sm[:, n % 4, 1:2], scale=ATTN_SCALE, accum_out=sm[:, n % 4, 2:3]).then_inc(s_exp, 1)

            def att_turned(n, probsT, bank):
                act.wait_ge(p_turned, n + 1)
                if n >= 2:
                    act.wait_ge(o_done, n - 1)
                cols = mask_cols[n // HEADS]
                act.activation(probsT[:, 0:cols], banks[:, bank, 0:cols], ACT.Copy).then_inc(p_out, 1)

            turns_out(TOKG - 1)
            for step in range(HEADS + 2):
                if step < HEADS:
                    att_exp(step, probs_first[:, step % 2, :])
                n = step - 2
                if n >= 0:
                    att_turned(n, probsT_first[:, n % 2, :], 4 + n % 2)
            split_mixed(0)
            for u in range(U_OUT + WSLOTS, U_QUERY):
                split_weights(0, u)
            act.wait_ge(y_out, 2)
            squares(NT, 0, 0, square)
            root(4, 1)
            for g in range(Q_GROUPS + 1):
                if g < Q_GROUPS:
                    act.wait_ge(w_used, U_QUERY + 4 * (g + 1))
                    if g >= 2:
                        act.wait_ge(qt_done, g - 1)
                    act.activation(qtok[:, g % 2, :], banks[:, g % 2, :], ACT.Copy).then_inc(q_out, 1)
                n = g - 1
                if n >= 0:
                    act.wait_ge(qt_done, n + 1)
                    if n >= 2:
                        act.wait_ge(k_done, n - 1)
                    act.activation(q2T0[:, n % 2, :], banks[:, 2 + n % 2, :], ACT.Copy).then_inc(qt_out, 1)
                if g == 2:
                    act.wait_ge(k_out, 1)
                    act.activation(sc.rearrange("p a n -> p (a n)"), scores[:, 0:2 * NKEY], ACT.Copy).then_inc(r_in, 1)
            act.wait_ge(r_max, 1)
            act.activation(gprob[:, 0, :], best, ACT.Exp, bias=gstat[:, 0:1], accum_out=gstat[:, 1:2]).then_inc(r_exp, 1)

            def split_weights2(r, u, loaded, n):
                act.wait_ge(loaded, r * 16 + 16 * (n + 1))
                if not isinstance(r, int):
                    act.nop(nofuse=True)
                full, (hi, lo) = slot_of(u)
                act.activation(hi, full, ACT.Copy).then_inc(w_split, 1)

            def side(g):
                ga = g - G_ATT
                for j in range(2):
                    n = HEADS + 2 * ga - 6 + j
                    if HEADS <= n < UNITS:
                        att_turned(n, probsT_side[:, j, :], 2 + j)
                for j in range(2):
                    n = HEADS + 2 * ga - 2 + j
                    if HEADS <= n < UNITS:
                        att_exp(n, probs_side[:, n % 4, :])
                for b in range(1, NT):
                    if ga == 4 * b + 3:
                        split_mixed(b)
                for q in OUT_SPLITS.get(g, ()):
                    split_weights2(0, U_OUT2 + q, wo2_in[q % 4], q // 4)
                if g == G_ADD + 1:
                    act.wait_ge(y_out, 2 * NT)
                    for b in range(1, NT):
                        squares(NT + b, b, b - 1, square2)
                if g == G_NORM:
                    root(5, NT - 1)
                if g == G_NORM + 1:
                    split_norm(range(1, NT), hn_block)

            def side_query_out(r, h, a):
                act.wait_ge(w_used, 2 * r + (U_QUERY2 + 2 * h + a + 1))
                act.wait_ge(k_done, 2 * r + (Q_GROUPS + 2 * h + a - 1))
                if not isinstance(r, int):
                    act.nop(nofuse=True)
                act.activation(q2T[:, a, :], banks[:, a, 0:SB], ACT.Copy).then_inc(q_out, 1)

            act.wait_ge(k_out, Q_GROUPS)
            act.wait_ge(xn_ready, 1)
            act.wait_ge(pad_set, 1)

            def experts(r, i):
                act.wait_ge(r_done, r + (i + 1))
                if PH - 1 <= i <= I_QUERY + PH:
                    act.wait_ge(k_out, 2 * r + (Q_GROUPS + 2 * (i + 1 - PH) + 2))
                act.nop(nofuse=True)
                act.activation(sc.rearrange("p a n -> p (a n)"),
                               scores[:, (i + 1) * 2 * NKEY:(i + 2) * 2 * NKEY] if isinstance(r, int) else
                               scores[:, bass.ds((r + (i + 1)) * (2 * NKEY), 2 * NKEY)], ACT.Copy).then_inc(r_in, 1)
                for q in range(4):
                    act.wait_ge(dot_done, r * PTOP + (i * PTOP + 4 * q + 4))
                    act.activation(gel[:, 4 * q:4 * q + 4], dots[:, 4 * q:4 * q + 4], ACT.Gelu).then_inc(gel_done, 1)
                    if q == 1:
                        act.wait_ge(r_max, r + (i + 2))
                        act.activation(gprob[:, (i + 1) % 2, :], best, ACT.Exp, bias=gstat[:, 0:1],
                                       accum_out=gstat[:, 1:2]).then_inc(r_exp, 1)
                    if i < I_QUERY:
                        side(4 * i + q)
                    elif i < I_QUERY + PH:
                        h = i - I_QUERY
                        if q in (1, 2):
                            side_query_out(r, h, q - 1)
                        if q in (0, 1):
                            split_weights2(r, U_QUERY2 + q, wq2_in[q], h)

            for_all_iterations(act, experts)

        @block.gpsimd
        def _(pool):
            pool.memset(scores[:, ITERS * 2 * NKEY:], 0.0).then_inc(pad_set, 1)
            pool.wait_ge(pad_set, 1)
            pool.memset(kiT[64:P], 0.0).then_inc(pad_set, 1)
            pool.wait_ge(pad_set, 2)
            pool.memset(kiT_low[0:64], 0.0).then_inc(pad_set, 1)

            pool.wait_ge(pad_set, 3)

            def rest_of_weights(t, u):
                pool.wait_ge(w_split, t + splits(u))
                full, (hi, lo) = slot_of(u)
                pool.tensor_tensor(lo, full, hi.bitcast(F32), ALU.subtract).then_inc(w_ready, 1)

            def rest_of_weight_loop(first, count):
                with pool.Fori(0, count // WSLOTS) as tt:
                    for s in range(WSLOTS):
                        rest_of_weights(tt * WSLOTS, first + s)

            def rest_of_norm():
                for b in range(1, NT):
                    for j in range(2):
                        pool.wait_ge(x_split, 2 * NT - 2 + 2 * b + j + 1)
                        piece = (slice(None), slice(4 * j, 4 * j + 4), slice(b * P, (b + 1) * P))
                        pool.tensor_tensor(hn_lo[piece], hn_full[piece], x_hi[piece].bitcast(F32), ALU.subtract).then_inc(x_ready, 1)

            def rest_of_mixed(b):
                pool.wait_ge(m_split, b + 1)
                tb = slice(b * P, (b + 1) * P)
                pool.tensor_tensor(mixed_lo[:, :, tb], mixed[:, :, tb], x_hi[:, :, tb].bitcast(F32), ALU.subtract).then_inc(m_ready, 1)

            for u in range(WSLOTS):
                rest_of_weights(0, u)
            rest_of_weight_loop(WSLOTS, U_OUT - 1)
            rest_of_weights(0, U_OUT + WSLOTS - 1)
            rest_of_mixed(0)
            for u in range(U_OUT + WSLOTS, U_QUERY):
                rest_of_weights(0, u)
            pool.wait_ge(g2row_in, 16)
            pool.wait_ge(n_turned, 2 * NT + 2)
            pool.tensor_tensor(xn0, xn0, g2row0, ALU.mult).then_inc(xn_ready, 1)

            def side(g):
                for b in range(1, NT):
                    if g - G_ATT == 4 * b + 3:
                        rest_of_mixed(b)
                for q in OUT_SPLITS.get(g, ()):
                    rest_of_weights(0, U_OUT2 + q)
                if g == G_NORM + 1:
                    rest_of_norm()
                if g == G_GAIN:
                    pool.wait_ge(g2again_in, 16)
                    for b in range(1, NT):
                        pool.wait_ge(n_turned, 2 * NT + 2 * b + 2)
                        pool.tensor_tensor(xn_tok[:, b, :], xn_tok[:, b, :], g2row, ALU.mult).then_inc(xn_ready, 1)

            pool.wait_ge(k_done, Q_GROUPS)
            pool.wait_ge(xn_ready, 1)

            def experts(r, i):
                pool.wait_ge(r_done, r + (i + 1))
                for k in range(PTOP):
                    pool.wait_ge(row_free, r * PTOP + (i * PTOP + k + 1))
                    pool.nop(nofuse=True)
                    pool.indirect_dma_start(slots[:, k % RING, :], None, uv,
                                            bass.IndirectOffsetOnAxis(eidx[:, i % 2, k:k + 1], 0)).then_inc(row_in[k % RING], 16)
                    if k % 4 == 3:
                        q = k // 4
                        if 0 <= 4 * i + q - 1 < 4 * I_QUERY:
                            side(4 * i + q - 1)
                        if I_QUERY <= i < I_QUERY + PH and q in (1, 2):
                            u = U_QUERY2 + 2 * (i - I_QUERY) + q - 1
                            pool.wait_ge(w_split, 2 * r + splits(u))
                            full, (hi, lo) = query_slots[q - 1]
                            pool.tensor_tensor(lo, full, hi.bitcast(F32), ALU.subtract).then_inc(w_ready, 1)

            for_all_iterations(pool, experts)

        @block.vector
        def _(dve):
            link = Link(dve, ch_dve)
            dve.nop(nofuse=True).then_inc(cv_done, 4)
            dve.wait_ge(const_in, 64)

            def inv_root(n, cols, width):
                dve.tensor_scalar(st[:, 1, 0:cols], st[:, 0, 0:cols], 1.0 / width, EPS, ALU.mult, ALU.add).then_inc(n_var, 1)
                dve.wait_ge(n_root, n + 1)
                link.then(dve.reciprocal(st[:, 3, 0:cols], st[:, 2, 0:cols]))
                link.then(dve.tensor_tensor(st[:, 4, 0:cols], st[:, 3, 0:cols], st[:, 3, 0:cols], ALU.mult))
                link.then(dve.tensor_tensor(st[:, 4, 0:cols], st[:, 4, 0:cols], st[:, 1, 0:cols], ALU.mult))
                link.then(dve.tensor_scalar(st[:, 4, 0:cols], st[:, 4, 0:cols], -0.5, 1.5, ALU.mult, ALU.add))
                link.then(dve.tensor_tensor(st[:, 3, 0:cols], st[:, 3, 0:cols], st[:, 4, 0:cols], ALU.mult))

            def norm_scale(b, col, dst):
                dve.tensor_scalar(dst, resid[:, b, :], st[:, 3, col:col + 1], None, ALU.mult).then_inc(n_scaled, 1)

            def norm_out(m0, full, gain, bank):
                for j in range(2):
                    dve.wait_ge(n_turned, m0 + j + 1)
                    dve.tensor_tensor(full[:, 4 * j:4 * j + 4, :], banks[:, bank + j, :].rearrange("p (c t) -> p c t", c=4),
                                      gain[:, 4 * j:4 * j + 4].unsqueeze(2).to_broadcast([P, 4, P]), ALU.mult).then_inc(n_out, 1)

            dve.wait_ge(n_sq, NT)
            inv_root(0, NT, D)
            for b in range(NT):
                norm_scale(b, b, xn_tok[:, b, :])
            dve.wait_ge(n_scaled, NT)
            for b in range(NT + 1):
                if b < NT:
                    norm_out(2 * b, xn_block(b), g1, 4)
                for j in range(2 if b >= 1 else 0):
                    dve.wait_ge(x_split, 2 * (b - 1) + j + 1)
                    piece = (slice(None), slice(4 * j, 4 * j + 4), slice((b - 1) * P, b * P))
                    dve.tensor_tensor(xn_lo[piece], xn_full[piece], x_hi[piece].bitcast(F32), ALU.subtract).then_inc(x_ready, 1)

            def rotate(x1, x2, cos, sin, shape):
                n = shape[1] * shape[2] * shape[3]
                c, s_ = (t.unsqueeze(2).to_broadcast(shape) for t in (cos, sin))
                tv = [turn[:, q, 0:n].rearrange("p (b h r) -> p b h r", b=shape[1], h=shape[2]) for q in range(4)]
                link(dve.tensor_tensor(tv[0], x1, c, ALU.mult))
                link(dve.tensor_tensor(tv[1], x2, s_, ALU.mult))
                link(dve.tensor_tensor(tv[2], x2, c, ALU.mult))
                link.then(dve.tensor_tensor(tv[3], x1, s_, ALU.mult))
                link(dve.tensor_tensor(x1, tv[0], tv[1], ALU.subtract))
                dve.tensor_tensor(x2, tv[2], tv[3], ALU.add).then_inc(tp_ready, 1)
                link.upto(link.count)

            def token_group(g):
                kind = TOK_KINDS[g]
                dve.wait_ge(tp_out, NT * (g + 1))
                if kind in ("ki", "kv"):
                    dve.wait_ge(part_out, {"ki": 2 * NT, "kv": 3 * NT + 1}[kind])
                if g > 0:
                    dve.wait_ge(tp_ready, g)
                if kind in ("kv", "q0", "q1"):
                    nh, gain = (2, 1) if kind == "kv" else (4, 0)
                    cols = NT * nh
                    r4 = raws[:, g % 2, :, 0:nh * HD].rearrange("p b (h c) -> p b h c", h=nh)
                    sq = head_sq[:, 0:cols * HD].rearrange("p (b h c) -> p b h c", b=NT, h=nh)
                    link.then(dve.tensor_tensor(sq, r4, r4, ALU.mult))
                    link.then(dve.tensor_reduce(st[:, 0, 0:cols], head_sq[:, 0:cols * HD].rearrange("p (n c) -> p n c", c=HD),
                                                AX.X, ALU.add))
                    inv_root(g - 1, cols, HD)
                    inv = st[:, 3, 0:cols].rearrange("p (b h) -> p b h", b=NT)
                    for b in range(NT):
                        rb = r4[:, b, :, :]
                        link(dve.tensor_tensor(rb, rb, inv[:, b, :].unsqueeze(2).to_broadcast([P, nh, HD]), ALU.mult))
                    link.upto(link.count)
                    for b in range(NT):
                        rb = r4[:, b, :, :]
                        link(dve.tensor_tensor(rb, rb, qk_gain[:, gain, :].unsqueeze(1).to_broadcast([P, nh, HD]), ALU.mult))
                    link.upto(link.count)
                    rotate(r4[:, :, :, 0:ROPE_Q], r4[:, :, :, ROPE_Q:2 * ROPE_Q], cos_q, sin_q, [P, NT, nh, ROPE_Q])
                else:
                    nh = IH if kind == "qi" else 2
                    r4 = raws[:, g % 2, :, 0:nh * ID].rearrange("p b (h c) -> p b h c", h=nh)
                    rotate(r4[:, :, :, 0:ROPE_I], r4[:, :, :, ROPE_I:2 * ROPE_I], cos_i, sin_i, [P, NT, nh, ROPE_I])

            for g in range(TOKG - 1):
                token_group(g)

            for b in range(1, NT):
                for h in range(IH):
                    n = IH * (b - 1) + h
                    dve.wait_ge(id_relu, n + 1)
                    r = relus[:, n % 2, 0:mask_cols[b]]
                    if h == 0:
                        dve.tensor_scalar(masks[b], r, wi[:, b, 0:1], None, ALU.mult).then_inc(id_used, 1)
                    else:
                        dve.wait_ge(id_used, n)
                        dve.scalar_tensor_tensor(masks[b], r, wi[:, b, h:h + 1], masks[b], ALU.mult, ALU.add).then_inc(id_used, 1)
                dve.wait_ge(id_used, IH * b)
                link(dve.tensor_tensor(masks[b][:, b * P:], masks[b][:, b * P:], tri, ALU.add))
            link.upto(link.count)
            token_group(TOKG - 1)
            for b in range(1, NT):
                for _ in range(TOPK_KEYS // 8):
                    link.then(dve.max(mx8, masks[b]))
                    link.then(dve.match_replace(masks[b], mx8, masks[b], TAKEN))
                link.then(dve.tensor_scalar(masks[b], masks[b], TAKEN / 2, MASKED, ALU.is_gt, ALU.mult))

            dve.wait_ge(tt_done, TURN0[-2])
            link.then(dve.memset(u_pad[:, :, 0:CONV_K - 1], 0.0))
            PER = 4 * 6
            with dve.Fori(0, KC // 4) as mm:
                m = mm * 4
                link.enter(mm, PER)
                for s in range(4):
                    dve.wait_ge(cp_out, m * 5 + (4 + 5 * s + 4))
                    w = taps[:, bass.ds(m + s, 1), :]
                    u = u_pad[:, s % 2, :]
                    link.then(dve.tensor_tensor(u[:, CONV_K - 1:], chan_sets[:, s, 0, :], chan_sets[:, s, 1, :], ALU.mult))
                    link.then(dve.tensor_scalar(conv, u[:, 0:SEQ], w[:, 0, 0:1], None, ALU.mult))
                    for j in range(1, CONV_K):
                        link.then(dve.scalar_tensor_tensor(conv, u[:, j:j + SEQ], w[:, 0, j:j + 1], conv, ALU.mult, ALU.add))
                    link.then(dve.tensor_tensor(conv, conv, chan_sets[:, s, 2, :], ALU.mult))
                    link.then(dve.tensor_tensor(mixed[:, bass.ds(m + s, 1), :].rearrange("p a t -> p (a t)"), conv,
                                                chan_sets[:, s, 3, :], ALU.mult))
                    dve.nop(nofuse=True).then_inc(cv_done, 1)
                link.leave(KC // 4)

            def att_max(n, probs, free):
                b = n // HEADS
                dve.wait_ge(s_done, n + 1)
                if free > 0:
                    dve.wait_ge(p_turned, free)
                cols = mask_cols[b]
                link.then(dve.tensor_tensor_reduce(out=probs[:, 0:cols], in0=banks[:, n % 2, 0:cols], in1=tri if b == 0 else masks[b],
                                                   scale=1.0, scalar=TAKEN, op0=ALU.add, op1=ALU.max,
                                                   accum_out=sm[:, n % 4, 0:1]))
                dve.tensor_scalar(sm[:, n % 4, 1:2], sm[:, n % 4, 0:1], -ATTN_SCALE, None, ALU.mult).then_inc(s_max, 1)

            def att_scale(n, probs):
                cols = mask_cols[n // HEADS]
                dve.wait_ge(s_exp, n + 1)
                link.then(dve.reciprocal(sm[:, n % 4, 3:4], sm[:, n % 4, 2:3]))
                dve.tensor_scalar(probs[:, 0:cols], probs[:, 0:cols], sm[:, n % 4, 3:4], None, ALU.mult).then_inc(s_prob, 1)

            def att_merge(n, acc, done):
                b, h = divmod(n, HEADS)
                dve.wait_ge(o_done, done)
                tb = slice(b * P, (b + 1) * P)
                link.then(dve.tensor_tensor(gate_b[:, h, tb], acc, gate_b[:, h, tb], ALU.mult))
                dve.tensor_tensor(mixed[:, h, tb], mixed[:, h, tb], gate_b[:, h, tb], ALU.add).then_inc(o_used, 1)

            for step in range(HEADS + 4):
                if step < HEADS:
                    att_max(step, probs_first[:, step % 2, :], step - 1)
                n = step - 1
                if 0 <= n < HEADS:
                    att_scale(n, probs_first[:, n % 2, :])
                n = step - 4
                if n >= 0:
                    if n == 0:
                        dve.wait_ge(cp_out, 4 + 5 * KC)
                    att_merge(n, banks[:, 2 + n % 2, 0:P], n + 1)

            def add_half(b, s, bank):
                half = resid[:, b, s * 512:(s + 1) * 512]
                dve.tensor_tensor(half, banks[:, bank, :], half, ALU.add).then_inc(y_out, 1)

            dve.wait_ge(x_again, 16)
            for s in range(2):
                dve.wait_ge(w_used, U_OUT + 4 * (s + 1))
                add_half(0, s, 6 + s)
            dve.wait_ge(n_sq, NT + 1)
            inv_root(4, 1, D)
            norm_scale(0, 0, xn0)
            norm_out(2 * NT, hn0, g2, 4)

            score4 = scores[:, 0:ITERS * 2 * NKEY].rearrange("p (b j n) -> p b j n", b=NT, j=2 * PH)

            def first_scores_out(n):
                dve.wait_ge(k_done, n + 1)
                dve.tensor_copy(scores[:, n * 512:(n + 1) * 512], banks[:, 4 + n % 2, :]).then_inc(k_out, 1)

            first_scores_out(0)

            def side(g):
                ga = g - G_ATT
                for j in range(2):
                    n = HEADS + 2 * ga - 4 + j
                    if HEADS <= n < UNITS:
                        att_scale(n, probs_side[:, n % 4, :])
                for j in range(2):
                    n = HEADS + 2 * ga - 2 + j
                    if HEADS <= n < UNITS:
                        att_max(n, probs_side[:, n % 4, :], n - 3 if n >= HEADS + 4 else 0)
                for j in range(2):
                    n = HEADS + 2 * ga - 8 + j
                    if HEADS <= n < UNITS:
                        att_merge(n, banks[:, 6, j * P:(j + 1) * P], n - j + 2)
                if g in (G_ADD, G_ADD + 1):
                    s = g - G_ADD
                    dve.wait_ge(w_used, U_OUT2 + 4 * (s + 1))
                    for b in range(1, NT):
                        add_half(b, s, ([0, 1, 2], [3, 6, 7])[s][b - 1])
                if g == G_NORM:
                    dve.wait_ge(n_sq, 2 * NT)
                    inv_root(5, NT - 1, D)
                    for b in range(1, NT):
                        norm_scale(b, b - 1, xn_tok[:, b, :])
                if g == G_NORM + 1:
                    for b, bank in ((1, 0), (2, 2), (3, 6)):
                        norm_out(2 * NT + 2 * b, hn_block(b), g2, bank)

            def side_scores_out(r, h, a):
                dve.wait_ge(k_done, 2 * r + (Q_GROUPS + 2 * h + a + 1))
                j = 2 * h + a
                src = banks[:, 2 + a, 0:SB].rearrange("p (b n) -> p b n", n=NKEY)
                if isinstance(r, int):
                    dst = score4[:, 1:, j, :]
                else:
                    dve.nop(nofuse=True)
                    dst = score4[:, 1:, bass.ds(2 * r + j, 1), :].rearrange("p b a n -> p b (a n)")
                dve.tensor_copy(dst, src).then_inc(k_out, 1)

            def route_keys():
                for a in range(2):
                    ta = link(dve.max(topv[:, a, 0:8], sc[:, a, :]))
                link.upto(ta)
                for a in range(2):
                    link(dve.max_index(topi[:, a, 0:8], topv[:, a, 0:8], sc[:, a, :]))
                    ta = link(dve.match_replace(sc_cut[:, a, :], topv[:, a, 0:8], sc[:, a, :], TAKEN))
                link.upto(ta)
                for a in range(2):
                    ta = link(dve.max(topv[:, a, 8:16], sc_cut[:, a, :]))
                link.upto(ta)
                for a in range(2):
                    ta = link(dve.max_index(topi[:, a, 8:16], topv[:, a, 8:16], sc_cut[:, a, :]))
                link.upto(ta)
                link(dve.tensor_copy(topif, topi))

            def route_pairs():
                link.then(dve.tensor_tensor(cand.rearrange("p (k n) -> p k n", k=PTOP),
                                            topv[:, 0, :].unsqueeze(2).to_broadcast([P, PTOP, PTOP]),
                                            topv[:, 1, :].unsqueeze(1).to_broadcast([P, PTOP, PTOP]), ALU.add))
                link.then(dve.max(best[:, 0:8], cand))
                link(dve.max_index(pos[:, 0:8], best[:, 0:8], cand))
                link.then(dve.match_replace(cand_cut, best[:, 0:8], cand, TAKEN))
                link.then(dve.max(best[:, 8:16], cand_cut))
                link(dve.max_index(pos[:, 8:16], best[:, 8:16], cand_cut))
                dve.tensor_scalar(gstat[:, 0:1], best[:, 0:1], -1.0, None, ALU.mult).then_inc(r_max, 1)
                link.upto(link.count)

            def route_experts(s, exps):
                link(dve.tensor_scalar(posij[:, 0, :], pos, 4, None, ALU.logical_shift_right))
                link.then(dve.tensor_scalar(posij[:, 1, :], pos, 15, None, ALU.bitwise_and))
                link.then(dve.tensor_copy(posf, posij))
                for a in range(2):
                    link(dve.tensor_tensor(onehot[:, a, :, :], posf[:, a, :].unsqueeze(2).to_broadcast([P, PTOP, PTOP]),
                                           iota.unsqueeze(1).to_broadcast([P, PTOP, PTOP]), ALU.is_equal))
                link.upto(link.count)
                for a in range(2):
                    link(dve.tensor_tensor(onehot[:, a, :, :], onehot[:, a, :, :],
                                           topif[:, a, :].unsqueeze(1).to_broadcast([P, PTOP, PTOP]), ALU.mult))
                link.upto(link.count)
                link.then(dve.tensor_reduce(chosen, onehot, AX.X, ALU.add))
                dve.wait_ge(r_exp, exps)
                link(dve.reciprocal(gstat[:, 2:3], gstat[:, 1:2]))
                link.then(dve.scalar_tensor_tensor(eidx[:, s, :], chosen[:, 0, :], float(NKEY), chosen[:, 1, :], ALU.mult, ALU.add))
                dve.tensor_scalar(gprob[:, s, :], gprob[:, s, :], gstat[:, 2:3], None, ALU.mult).then_inc(r_done, 1)

            dve.nop(nofuse=True).then_inc(acc_free, 2)
            dve.wait_ge(r_in, 1)
            route_keys()
            route_pairs()
            route_experts(0, 1)
            link.upto(link.count)
            for n in range(1, Q_GROUPS):
                first_scores_out(n)
            ROUTE_LINKS = 11 + 6 + 10

            def experts(r, i):
                token = xn0 if i < PH else xn_tok[:, i // PH, :]
                if i == PH:
                    dve.wait_ge(xn_ready, NT)
                for q in range(4):
                    for k in range(4 * q, 4 * q + 4):
                        n = i * PTOP + k
                        dve.wait_ge(row_in[k % RING], r * 32 + 16 * (2 * i + k // RING + 1))
                        if n >= 2 and k % 4 >= 2 or k == 0 and i >= 1:
                            dve.wait_ge(dot_done, r * PTOP + (n - (1 if k else 0)))
                        dve.tensor_tensor_reduce(out=dotjunk(i, k), in0=slots[:, k % RING, 0:D], in1=token,
                                                 scale=1.0, scalar=0.0, op0=ALU.mult, op1=ALU.add,
                                                 accum_out=dots[:, k:k + 1]).then_inc(dot_done, 1)
                    dve.wait_ge(gel_done, r * 4 + (4 * i + q + 1))
                    if q == 0:
                        dve.wait_ge(r_done, r + (i + 1))
                    for k in range(4 * q, 4 * q + 4):
                        n = i * PTOP + k
                        dve.wait_ge(row_free, r * PTOP + (n + 1 + RING - DIAGS))
                        dve.tensor_scalar(diag[:, k % DIAGS, :], ident, gel[:, k:k + 1], gprob[:, i % 2, k:k + 1],
                                          ALU.mult, ALU.mult).then_inc(diag_done, 1)
                    if q == 0:
                        dve.wait_ge(r_in, r + (i + 2))
                        dve.nop(nofuse=True)
                        route_keys()
                    if q == 1:
                        link.upto(link.count)
                        route_pairs()
                        route_experts((i + 1) % 2, r + (i + 2))
                    if i < I_QUERY:
                        side(4 * i + q)
                    elif i < I_QUERY + PH and q >= 2:
                        side_scores_out(r, i - I_QUERY, q - 2)
                dve.wait_ge(row_free, r * PTOP + (PTOP * (i + 1) + RING))
                pair = i % 2 if i >= I_QUERY else 0
                blk = resid[:, i // PH, :].rearrange("p (h c) -> p h c", h=2)
                dve.wait_ge(acc_free, r + (i + 2))
                dve.tensor_tensor(blk, banks[:, 4 + 2 * pair:6 + 2 * pair, :], blk, ALU.add).then_inc(acc_free, 1)

            for_all_iterations(dve, experts, lambda rr: link.enter(rr, 2 * ROUTE_LINKS), link.leave)


def kernel(x, norm1_g, w_in, conv_w, q_norm_g, k_norm_g, w_o, norm2_g, peer_wq, peer_k1, peer_k2, peer_u, peer_v):
    import numpy as np
    import concourse.bacc as bacc
    from concourse.bass_utils import run_bass_kernel_spmd

    a = {k: np.asarray(v) for k, v in dict(
        x=x, norm1_g=norm1_g, w_in=w_in, conv_w=conv_w, q_norm_g=q_norm_g, k_norm_g=k_norm_g, w_o=w_o, norm2_g=norm2_g,
        peer_wq=peer_wq, peer_k1=peer_k1, peer_k2=peer_k2, peer_u=peer_u, peer_v=peer_v).items()}

    def chunks(w, cols):
        n = w.shape[1] // cols
        return np.ascontiguousarray(w.reshape(KC, P, n, cols).transpose(2, 1, 0, 3)).reshape(n, P, KC * cols)

    w = a["w_in"]
    tok = w[:, 3 * D:]
    n_tok = D + 2 * KVH * HD + IH * ID
    small = ID + IH
    ga0 = 3 * D + n_tok + small
    sel = [w[:, D:2 * D], w[:, 2 * D:3 * D], w[:, 0:D], w[:, ga0:ga0 + D], w[:, ga0 + D:ga0 + 2 * D]]
    w_chan = np.stack([chunks(s, P) for s in sel], axis=1).reshape(5 * KC, P, UNIT)

    def halves(w):
        return chunks(w, 512).reshape(-1, P, 4, UNIT).transpose(0, 2, 1, 3).reshape(-1, P, UNIT)

    kv1 = D + 2 * KVH * HD
    padded = np.pad(tok[:, n_tok:n_tok + small], ((0, 0), (0, P - small)))
    w_units = np.concatenate([halves(tok[:, kv1:n_tok]), chunks(padded, P), halves(tok[:, D:kv1]), halves(tok[:, 0:D]), w_chan, halves(a["w_o"]),
                              halves(a["peer_wq"]), chunks(a["peer_wq"], P)])

    t = np.arange(SEQ, dtype=np.float32)[:, None]

    def table(fn, half):
        inv = (np.float32(500000.0) ** (-np.arange(half, dtype=np.float32) / np.float32(half))).astype(np.float32)
        v = fn((t * inv[None, :]).astype(np.float32).astype(np.float64)).astype(np.float32)
        return v.reshape(NT, P, half).transpose(1, 0, 2).reshape(P, NT * half)

    lower = np.where(np.arange(P)[None, :] <= np.arange(P)[:, None], 0.0, MASKED).astype(np.float32)
    consts = np.concatenate([np.eye(P, dtype=np.float32), lower, np.tile(np.arange(16, dtype=np.float32), (P, 1)),
                             table(np.cos, ROPE_Q), table(np.sin, ROPE_Q), table(np.cos, ROPE_I), table(np.sin, ROPE_I)], axis=1)
    params = np.concatenate([a["norm1_g"].reshape(KC, P).T, a["norm2_g"].reshape(KC, P).T,
                             a["conv_w"].reshape(CONV_K, KC, P).transpose(2, 1, 0).reshape(P, KC * CONV_K)], axis=1)
    arrays = {
        "x": a["x"].reshape(SEQ, D),
        "w_units": w_units,
        "keys_t": np.ascontiguousarray(np.stack([a["peer_k1"], a["peer_k2"]], axis=1).transpose(0, 1, 3, 2)).reshape(2 * PH, P, NKEY),
        "uv": np.concatenate([a["peer_u"], a["peer_v"]], axis=1),
        "consts": consts,
        "params": params,
        "rows": np.concatenate([a["norm2_g"], a["q_norm_g"], a["k_norm_g"]]),
    }
    arrays = {k: np.ascontiguousarray(v) for k, v in arrays.items()}
    nc = bacc.Bacc("TRN2", target_bir_lowering=False, num_devices=1)
    args = [nc.dram_tensor("in_" + k, v.shape, F32, kind="ExternalInput").ap() for k, v in arrays.items()]
    out = nc.dram_tensor("out_h", (SEQ, D), F32, kind="ExternalOutput").ap()
    build(nc, *args, out)
    r = run_bass_kernel_spmd(nc, [{"in_" + k: v for k, v in arrays.items()}], core_ids=[0])
    return r.results[0]["out_h"].reshape(1, SEQ, D)
```

```python
from contextlib import ExitStack

import concourse.bass as bass
from concourse import mybir

ALU = mybir.AluOpType
ACT = mybir.ActivationFunctionType
AX = mybir.AxisListType
F32 = mybir.dt.float32
FR = mybir.dt.float32r
U32 = mybir.dt.uint32

P = 128
SEQ, D = 512, 1024
NT = SEQ // P
KC = D // P
HEADS, HD, KVH = 8, 128, 2
GROUP = HEADS // KVH
IH, ID = 8, 64
TOPK_KEYS = min(256, SEQ // 4)
PH, NKEY, PTOP = 8, 128, 16
CONV_K = 3
EPS = 1e-6
ATTN_SCALE = HD ** -0.5
IDX_SCALE = ID ** -0.5
IDX_W_SCALE = IH ** -0.5
ROPE_Q, ROPE_I = HD // 4 // 2, ID // 4 // 2
MASKED = -1.0e30
TAKEN = -3.0e38
RING = 8
DIAGS = 4
UNITS = NT * HEADS
ITERS = NT * PH
CONST_COLS = 128 + 128 + 16 + 2 * NT * ROPE_Q + 2 * NT * ROPE_I
WSLOTS = 4
UNIT = KC * P
TOK_KINDS = ("qi", "kv", "q0", "q1")
TOK_START = (0, 5, 9, 13)
U_KI = 4
TURNS = {"qi": 4, "kv": 2, "ki": 1, "q0": 4, "q1": 4}
TURN0 = {"qi": 0, "kv": 4, "ki": 6, "q0": 7, "q1": 11, "end": 15}
U_CHAN = TOK_START[-1] + 4
U_OUT = U_CHAN + 5 * KC
U_QUERY = U_OUT + 2 * D // 512 * 2
U_OUT2 = U_QUERY + 2 * PH
U_QUERY2 = U_OUT2 + 8
G_ATT = 0
G_OUT = 16
OUT_SPLITS = {G_OUT - 1: (0, 1), G_OUT: (2, 3), G_OUT + 2: (4, 5), G_OUT + 3: (6, 7)}
G_ADD = G_OUT + 3
G_NORM = G_OUT + 5
G_GAIN = G_NORM + 1
I_QUERY = 6
PARAM_COLS = KC + KC + KC * CONV_K


class Link:

    def __init__(self, eng, sem):
        self.eng, self.sem, self.count, self.var, self.per = eng, sem, 0, None, 0

    def __call__(self, ins):
        ins.then_inc(self.sem, 1)
        self.count += 1
        return self.count

    def upto(self, count):
        if self.var is None:
            self.eng.wait_ge(self.sem, count)
        else:
            self.eng.wait_ge(self.sem, self.var * self.per + count)
            self.eng.nop(nofuse=True)

    def then(self, ins):
        self.upto(self(ins))

    def enter(self, var, per):
        self.var, self.per, self.start = var, per, self.count

    def leave(self, trips):
        assert self.count - self.start == self.per, (self.count - self.start, self.per)
        self.count, self.var = self.start + trips * self.per, None


def build(nc, x, w_units, keys_t, uv, consts, params, rows, out):
    with ExitStack() as ctx:
        def sb(name, cols, dt=F32):
            return ctx.enter_context(nc.sbuf_tensor(name, [P, cols], dt))

        def sem(name):
            return ctx.enter_context(nc.semaphore(name))

        banks = ctx.enter_context(nc.psum_tensor("banks", [P, 8, 512], F32))
        regions = dict(ring=RING * 2 * D, xreg=KC * SEQ, resid=NT * D, qreg=HEADS * SEQ, mreg=KC * SEQ, big=(ITERS + 1) * 2 * NKEY)
        arena = sb("arena", sum(regions.values()))[:]
        arena_start = nc.sbuf_base - 4 * sum(regions.values())
        at, region = 0, {}
        for name, cols in regions.items():
            region[name] = (at, cols)
            at += cols

        def part(name):
            return arena[:, region[name][0]:region[name][0] + region[name][1]]

        def rounded(name, where, col, cols):
            return nc.alloc_sbuf_tensor_at(name, [P, cols], FR, offset=arena_start + 4 * (region[where][0] + col), align_bytes=32)[:]

        resid = part("resid").rearrange("p (b d) -> p b d", b=NT)
        tokmaj = sb("tokmaj", NT * D)[:]
        xn_tok = tokmaj.rearrange("p (b d) -> p b d", b=NT)
        gate_b = tokmaj.rearrange("p (m t) -> p m t", m=KC)
        x_hi = rounded("x_hi", "xreg", 0, KC * SEQ).rearrange("p (k t) -> p k t", k=KC)
        xn_full = part("resid").rearrange("p (k t) -> p k t", k=KC)
        xn_lo = rounded("xn_lo", "resid", 0, KC * SEQ).rearrange("p (k t) -> p k t", k=KC)
        hn_full = part("qreg").rearrange("p (k t) -> p k t", k=KC)
        hn_lo = rounded("hn_lo", "qreg", 0, KC * SEQ).rearrange("p (k t) -> p k t", k=KC)
        xn0 = sb("xn0", D)[:]
        big = part("big")
        scores = big
        chan_sets = big[:, 0:4 * 4 * SEQ].rearrange("p (s q t) -> p s q t", s=4, q=4)
        square = big[:, 0:D]
        square2 = part("qreg")[:, 0:D]
        ring = part("ring")
        slots = ring.rearrange("p (r e) -> p r e", r=RING)

        def slot(k):
            return (k + 2) % RING

        w_full = ring[:, 0:WSLOTS * UNIT].rearrange("p (s e) -> p s e", s=WSLOTS)
        w_lo = rounded("w_lo", "ring", 0, WSLOTS * UNIT).rearrange("p (s e) -> p s e", s=WSLOTS)
        w_hi = rounded("w_hi", "ring", WSLOTS * UNIT, WSLOTS * UNIT).rearrange("p (s e) -> p s e", s=WSLOTS)
        rest = 2 * WSLOTS * UNIT
        raws = ring[:, rest:rest + 2 * NT * 512].rearrange("p (s b c) -> p s b c", s=2, b=NT)
        tail = ring[:, rest + 2 * NT * 512:]
        relus = tail[:, 0:2 * SEQ].rearrange("p (s t) -> p s t", s=2)
        SIDE0 = PH * 2 * NKEY
        ki_chan = relus[:, 0, :]
        ki_raw = relus[:, 1, :].rearrange("p (b c) -> p b c", b=NT)
        probs_first = tail[:, 2 * SEQ:4 * SEQ].rearrange("p (s t) -> p s t", s=2)
        probs_side = big[:, SIDE0:SIDE0 + 4 * SEQ].rearrange("p (s t) -> p s t", s=4)
        probsT_side = big[:, SIDE0 + 4 * SEQ:SIDE0 + 6 * SEQ].rearrange("p (s t) -> p s t", s=2)
        junk_early = big[:, SIDE0 + 8 * SEQ:SIDE0 + 8 * SEQ + 2 * D].rearrange("p (s d) -> p s d", s=2)
        g2row0 = ring[:, rest + NT * 512:rest + NT * 512 + D]
        key0 = ring[:, rest + NT * 512 + D:rest + NT * 512 + D + 2 * PH * NKEY].rearrange("p (j n) -> p j n", n=NKEY)
        free = rest + 2 * NT * 512 + 4 * SEQ
        q2T0 = ring[:, free + D:free + D + 4 * P].rearrange("p (s t) -> p s t", s=4)
        kiT_low = ring[:, free:free + SEQ]
        hn0 = ring[:, free:free + D].rearrange("p (k t) -> p k t", k=KC)

        def xn_block(b):
            return xn_full[:, :, b * P:(b + 1) * P]

        def hn_block(b):
            return hn0 if b == 0 else hn_full[:, :, b * P:(b + 1) * P]

        def splits(u):
            return u + 1 - (U_OUT2 - U_QUERY if u >= U_OUT2 else 0)

        def lo_parts(u):
            return splits(u) - (4 if u >= U_OUT2 else 0)

        def unit_slot(name, where, col):
            full = part(where)[:, col:col + UNIT]
            return full, (rounded(name + "_hi", where, col + UNIT, UNIT), rounded(name + "_lo", where, col, UNIT))

        out_slots = [unit_slot(f"wo{s}", ("qreg", "big")[s // 2], SIDE0 * (s // 2) + 2 * UNIT * (s % 2)) for s in range(4)]
        query_slots = [unit_slot(f"wq{s}", "mreg", 2 * UNIT * s) for s in range(2)]

        out0_slots = [unit_slot(f"wo_first{s}", "big", 2 * UNIT * s) for s in range(4)]

        def slot_of(u):
            if U_OUT + WSLOTS <= u < U_QUERY:
                return out0_slots[u - U_OUT - WSLOTS]
            if u < U_OUT2:
                s = u % WSLOTS
                return w_full[:, s, :], (w_hi[:, s, :], w_lo[:, s, :])
            return out_slots[(u - U_OUT2) % 4] if u < U_QUERY2 else query_slots[(u - U_QUERY2) % 2]

        UP = SEQ + CONV_K - 1
        u_pad = raws[:, 0, :, :].rearrange("p b c -> p (b c)")[:, 0:2 * UP].rearrange("p (s t) -> p s t", s=2)
        conv = raws[:, 0, :, :].rearrange("p b c -> p (b c)")[:, 2 * UP:2 * UP + SEQ]
        qT = part("qreg").rearrange("p (h t) -> p h t", h=HEADS)
        kreg = sb("kreg", KVH * SEQ)[:]
        kT = kreg.rearrange("p (h t) -> p h t", h=KVH)
        g2row = kreg
        SB = SEQ - P
        q2T = kreg[:, 0:2 * SB].rearrange("p (s t) -> p s t", s=2)
        vreg = sb("vreg", NT * KVH * HD)[:]
        v_tok = vreg.rearrange("p (b c) -> p b c", b=NT)
        key_sb = vreg[:, 0:4 * NKEY].rearrange("p (s e) -> p s e", s=2)
        ireg = sb("ireg", 4 * SEQ)[:]
        qiT = ireg.rearrange("p (h t) -> p h t", h=4)
        probsT_first = ireg[:, 0:2 * SEQ].rearrange("p (s t) -> p s t", s=2)
        sc = ireg[:, 0:256].rearrange("p (a n) -> p a n", a=2)
        sc_cut = ireg[:, 256:512].rearrange("p (a n) -> p a n", a=2)
        cand = ireg[:, 512:768]
        cand_cut = ireg[:, 768:1024]
        onehot = ireg[:, 1024:1536].rearrange("p (a k n) -> p a k n", a=2, k=PTOP)
        diag = ireg[:, 1536:2048].rearrange("p (s n) -> p s n", s=DIAGS)
        kiT = sb("kiT", SEQ)[:]
        mreg = part("mreg")
        mixed = mreg.rearrange("p (m t) -> p m t", m=KC)
        mixed_lo = rounded("mixed_lo", "mreg", 0, KC * SEQ).rearrange("p (m t) -> p m t", m=KC)
        head_sq = mreg[:, 0:NT * 512]
        turn = mreg[:, NT * 512:NT * 512 + 4 * NT * 4 * ROPE_Q].rearrange("p (q n) -> p q n", q=4)
        junk_late = mreg[:, 0:2 * D].rearrange("p (s d) -> p s d", s=2)
        mask_cols = [P * (b + 1) for b in range(NT)]
        mask_at = [sum(mask_cols[1:b]) for b in range(NT)]
        maskreg = sb("maskreg", sum(mask_cols[1:]))[:]
        masks = [maskreg[:, mask_at[b]:mask_at[b] + mask_cols[b]] for b in range(NT)]

        def dotjunk(i, k):
            if i < G_OUT // 4:
                return junk_early[:, k % 2, :]
            if i < I_QUERY + PH:
                return (maskreg[:, 0:D], xn_tok[:, 0, :])[k % 2]
            return junk_late[:, k % 2, :]
        cst = sb("cst", CONST_COLS)[:]
        ident, tri, iota = cst[:, 0:128], cst[:, 128:256], cst[:, 256:272]
        at = 272
        tables = []
        for half in (ROPE_Q, ROPE_Q, ROPE_I, ROPE_I):
            tables.append(cst[:, at:at + NT * half].rearrange("p (b r) -> p b r", b=NT))
            at += NT * half
        cos_q, sin_q, cos_i, sin_i = tables
        par = sb("par", PARAM_COLS)[:]
        g1, g2 = par[:, 0:KC], par[:, KC:2 * KC]
        taps = par[:, 2 * KC:].rearrange("p (m j) -> p m j", j=CONV_K)
        qk_gain = sb("qk_gain", 2 * HD)[:].rearrange("p (a c) -> p a c", a=2)
        wi = sb("wi", NT * IH)[:].rearrange("p (b h) -> p b h", b=NT)
        st = sb("st", 5 * 16)[:].rearrange("p (a n) -> p a n", a=5)
        mx8 = sb("mx8", 8)[:]
        sm = sb("sm", 16)[:].rearrange("p (s a) -> p s a", s=4)
        topv = kiT[:, 0:2 * PTOP].rearrange("p (a k) -> p a k", a=2)
        topi = sb("topi", 2 * PTOP, U32)[:].rearrange("p (a k) -> p a k", a=2)
        topif = kiT[:, 2 * PTOP:4 * PTOP].rearrange("p (a k) -> p a k", a=2)
        best = kiT[:, 12 * PTOP:13 * PTOP]
        pos = sb("pos", PTOP, U32)[:]
        posij = sb("posij", 2 * PTOP, U32)[:].rearrange("p (a k) -> p a k", a=2)
        posf = kiT[:, 4 * PTOP:6 * PTOP].rearrange("p (a k) -> p a k", a=2)
        chosen = kiT[:, 6 * PTOP:8 * PTOP].rearrange("p (a k) -> p a k", a=2)
        eidx = sb("eidx", 2 * PTOP, U32)[:].rearrange("p (s k) -> p s k", s=2)
        gprob = kiT[:, 8 * PTOP:10 * PTOP].rearrange("p (s k) -> p s k", s=2)
        gstat = sb("gstat", 3)[:]
        dots = kiT[:, 10 * PTOP:11 * PTOP]
        gel = kiT[:, 11 * PTOP:12 * PTOP]

        const_in = sem("const_in")
        x_in = [sem(f"x_in{b}") for b in range(NT)]
        x_again = sem("x_again")
        w_in = [sem(f"w_in{s}") for s in range(WSLOTS)]
        g2row_in = sem("g2row_in")
        key_in = sem("key_in")
        w_split = sem("w_split")
        w_ready = sem("w_ready")
        w_ready0 = sem("w_ready0")
        w_used = sem("w_used")
        x_split = sem("x_split")
        x_ready = sem("x_ready")
        wo0_in = [sem(f"wo0_in{s}") for s in range(4)]
        wo2_in = [sem(f"wo2_in{s}") for s in range(4)]
        wq2_in = [sem(f"wq2_in{s}") for s in range(2)]
        g2again_in = sem("g2again_in")
        key2_in = [sem(f"key2_in{s}") for s in range(2)]
        m_split = sem("m_split")
        m_ready0 = [sem(f"m_ready0{t}") for t in range(2)]
        m_ready = sem("m_ready")
        n_sq = sem("n_sq")
        n_var = sem("n_var")
        n_root = sem("n_root")
        n_scaled = sem("n_scaled")
        n_turned = sem("n_turned")
        n_out = sem("n_out")
        tp_done = sem("tp_done")
        tp_out = sem("tp_out")
        tp_ready = sem("tp_ready")
        ki_out = sem("ki_out")
        ki_back = sem("ki_back")
        ki_tok = sem("ki_tok")
        tt_done = sem("tt_done")
        tt_out = sem("tt_out")
        id_done = sem("id_done")
        id_relu = sem("id_relu")
        id_used = sem("id_used")
        cp_out = sem("cp_out")
        cv_done = sem("cv_done")
        s_done = sem("s_done")
        s_max = sem("s_max")
        s_exp = sem("s_exp")
        s_inv = sem("s_inv")
        s_prob = sem("s_prob")
        p_turned = sem("p_turned")
        p_out = sem("p_out")
        o_done = sem("o_done")
        o_used = sem("o_used")
        y_out = sem("y_out")
        xn_ready = sem("xn_ready")
        q_out = sem("q_out")
        k_done = sem("k_done")
        k_out = sem("k_out")
        r_in = sem("r_in")
        r_max = sem("r_max")
        r_exp = sem("r_exp")
        r_done = sem("r_done")
        row_in = [sem(f"row_in{s}") for s in range(RING)]
        dot_done = sem("dot_done")
        gel_done = sem("gel_done")
        diag_done = sem("diag_done")
        row_free = sem("row_free")
        acc_free = sem("acc_free")
        out_in = sem("out_in")
        part_out = sem("part_out")
        pad_set = sem("pad_set")
        ch_dve = sem("ch_dve")

        block = ctx.enter_context(nc.Block())

        def gelu_groups(i, q):
            return [[k] for k in range(4 * q, 4 * q + 4)] if i == ITERS - 1 and q == 3 else [list(range(4 * q, 4 * q + 4))]

        def for_all_iterations(eng, body, enter=None, leave=None):
            for i in range(PH):
                body(0, i)
            loops = [(PH, I_QUERY)] + [(b * PH, PH) for b in range(2, NT - 1)] + [((NT - 1) * PH, PH - 2)]
            for first, count in loops:
                with eng.Fori(0, count // 2) as rr:
                    if enter:
                        enter(rr)
                    for s in range(2):
                        body(rr * 2, first + s)
                    if leave:
                        leave(count // 2)
                for i in range(first + count, (first // PH + 1) * PH):
                    body(0, i)

        @block.sync
        def _(sp):
            sp.dma_start(cst, consts).then_inc(const_in, 16)
            for b in range(NT):
                sp.dma_start(resid[:, b, :], x[b * P:(b + 1) * P, :]).then_inc(x_in[b], 16)
                if b == 0:
                    sp.dma_start(par, params).then_inc(const_in, 16)
                    sp.dma_start(qk_gain[:, 0, :], rows[D:D + HD].partition_broadcast(P)).then_inc(const_in, 16)
                    sp.dma_start(qk_gain[:, 1, :], rows[D + HD:D + 2 * HD].partition_broadcast(P)).then_inc(const_in, 16)

            def fetch(u0, u):
                unit = w_units[u] if isinstance(u0, int) else w_units[bass.ds(u0 + u, 1)].rearrange("a p e -> p (a e)")
                done = wo0_in[u - U_OUT - WSLOTS] if U_OUT + WSLOTS <= u < U_QUERY else w_in[u % WSLOTS]
                sp.dma_start(slot_of(u)[0], unit).then_inc(done, 16)

            def fetch_next(first, count):
                with sp.Fori(0, count // WSLOTS) as tt:
                    t = tt * WSLOTS
                    for s in range(WSLOTS):
                        sp.wait_ge(w_used, t + (first + s - WSLOTS + 1))
                        fetch(t, first + s)
                for u in range(first + count - count % WSLOTS, first + count):
                    sp.wait_ge(w_used, u - WSLOTS + 1)
                    fetch(0, u)

            for u in range(WSLOTS):
                fetch(0, u)
            fetch_next(WSLOTS, U_OUT)
            for s in range(4):
                sp.wait_ge(cv_done, 4 + KC - 3 + s)
                fetch(0, U_OUT + WSLOTS + s)
            sp.dma_start(resid, x.rearrange("(b p) d -> p b d", p=P)).then_inc(x_again, 16)
            sp.wait_ge(tt_done, TURN0["end"])
            sp.wait_ge(id_used, 8 * (NT - 1))
            sp.dma_start(g2row0, rows[0:D].partition_broadcast(P)).then_inc(g2row_in, 16)
            sp.dma_start(key0, keys_t.rearrange("j p n -> p j n")).then_inc(key_in, 16)
            for u in range(U_QUERY, U_QUERY + WSLOTS):
                sp.wait_ge(w_used, u - 2 * WSLOTS + 1)
                fetch(0, u)
            fetch_next(U_QUERY + WSLOTS, 2 * PH - WSLOTS)

            def fetch2(src, u):
                unit = w_units[src] if isinstance(src, int) else w_units[bass.ds(src, 1)].rearrange("a p e -> p (a e)")
                done = wo2_in[(u - U_OUT2) % 4] if u < U_QUERY2 else wq2_in[(u - U_QUERY2) % 2]
                sp.dma_start(slot_of(u)[0], unit).then_inc(done, 16)

            def fetch_keys(h, s):
                src = keys_t[bass.ds(2 * h, 2)].rearrange("j p n -> p j n")
                sp.dma_start(key_sb[:, s, :].rearrange("p (j n) -> p j n", j=2), src).then_inc(key2_in[s], 16)

            sp.wait_ge(s_done, UNITS)
            fetch2(U_OUT, U_OUT2)
            fetch2(U_OUT + 1, U_OUT2 + 1)
            sp.dma_start(g2row, rows[0:D].partition_broadcast(P)).then_inc(g2again_in, 16)
            sp.wait_ge(o_done, UNITS)
            for q in range(2, 8):
                if q >= 4:
                    sp.wait_ge(w_used, U_OUT2 + q - 3)
                fetch2(U_OUT + q, U_OUT2 + q)
            fetch_keys(0, 0)
            fetch_keys(1, 1)
            sp.wait_ge(w_used, U_QUERY2)
            fetch2(U_QUERY, U_QUERY2)
            fetch2(U_QUERY + 1, U_QUERY2 + 1)

            def fetch_head(r, h):
                for a in range(2):
                    sp.wait_ge(w_used, 2 * r + (U_QUERY2 + 2 * h + a - 1))
                    fetch2(2 * r + (U_QUERY + 2 * h + a), U_QUERY2 + a)
                if not (isinstance(r, int) and r + h == PH - 1):
                    sp.wait_ge(k_done, 2 * r + (PH + 2 * h))
                    fetch_keys(r + (h + 1), (h + 1) % 2)

            with sp.Fori(0, PH // 2 - 1) as rr:
                fetch_head(rr * 2, 1)
                fetch_head(rr * 2, 2)
            fetch_head(0, PH - 1)
            out_blocks = out.rearrange("(b p) d -> p b d", p=P)
            sp.wait_ge(row_in[slot(PTOP - 1)], 16 * ITERS * PTOP // RING)
            sp.wait_ge(acc_free, 2 + PH * (NT - 1))
            sp.dma_start(out_blocks[:, 0:NT - 1, :], resid[:, 0:NT - 1, :]).then_inc(out_in, 16)
            sp.wait_ge(acc_free, 2 + ITERS)
            sp.dma_start(out_blocks[:, NT - 1, :], resid[:, NT - 1, :]).then_inc(out_in, 16)
            sp.wait_ge(out_in, 32)

        @block.tensor
        def _(pe):
            def turn_block(src, scaled, m0, bank, waits=False):
                pe.wait_ge(n_scaled, scaled)
                for j in range(2):
                    if waits:
                        pe.wait_ge(n_out, m0 + j - 1)
                    for c in range(4):
                        ins = pe.transpose(banks[:, bank + j, c * P:(c + 1) * P],
                                           src[:, (4 * j + c) * P:(4 * j + c + 1) * P], ident)
                    ins.then_inc(n_turned, 1)

            def split_product(out, w, x, first, last):
                pe.matmul(out, w[0], x[0], start=first, stop=False)
                pe.matmul(out, w[0], x[1], start=False, stop=False)
                return pe.matmul(out, w[1], x[0], start=False, stop=last)

            def unit_parts(u, k):
                return [w.rearrange("p (k c) -> p k c", k=k) for w in slot_of(u)[1]]

            pe.nop(nofuse=True).then_inc(row_free, RING)
            pe.wait_ge(const_in, 64)
            for b in range(NT):
                turn_block(xn_tok[:, b, :], b + 1, 2 * b, 4, b > 0)

            def token_projection(g):
                for q in range(4):
                    u = TOK_START[g] + q
                    pe.wait_ge(w_ready, u + 1)
                    wh, wl = unit_parts(u, 2)
                    for b in range(NT):
                        n = NT * g + b
                        tb = slice(b * P, (b + 1) * P)
                        if g == 0 and q == 0:
                            pe.wait_ge(x_ready, 2 * b + 2)
                        if q == 0 and g >= 1:
                            pe.wait_ge(tp_out, n - 3)
                        for c in range(2):
                            k = 2 * q + c
                            ins = split_product(banks[:, b, :], (x_hi[:, k, tb], xn_lo[:, k, tb]),
                                                (wh[:, c, :], wl[:, c, :]), k == 0, k == KC - 1)
                        if b == NT - 1:
                            ins.then_inc(w_used, 1)
                        elif q == 3:
                            ins.then_inc(tp_done, 1)

            def token_turns(kind):
                pe.wait_ge(tp_ready, list(TURNS).index(kind) + 1)
                for j in range(TURNS[kind]):
                    m = TURN0[kind] + j
                    if m >= 2:
                        pe.wait_ge(tt_out, m - 1)
                    for b in range(NT):
                        src = ki_raw[:, b, :] if kind == "ki" else raws[:, TOK_KINDS.index(kind) % 2, b, j * P:(j + 1) * P]
                        ins = pe.transpose(banks[:, 4 + m % 2, b * P:(b + 1) * P], src, ident)
                    ins.then_inc(tt_done, 1)

            for g, kind in enumerate(TOK_KINDS):
                token_projection(g)
                if kind == "qi":
                    pe.wait_ge(w_ready, U_KI + 1)
                    wh, wl = unit_parts(U_KI, KC)
                    for k in range(KC):
                        ins = split_product(banks[:, 6, :], (wh[:, k, :], wl[:, k, :]), (x_hi[:, k, :], xn_lo[:, k, :]),
                                            k == 0, k == KC - 1)
                    ins.then_inc(w_used, 1)
                if kind == "kv":
                    token_turns("qi")
                    pe.wait_ge(ki_out, 1)
                    for b in range(NT):
                        ins = pe.transpose(banks[:, 7, b * P:(b + 1) * P], ki_chan[:, b * P:(b + 1) * P], ident)
                    ins.then_inc(ki_back, 1)
                if kind == "q0":
                    token_turns("kv")
                    token_turns("ki")
                if kind == "q1":
                    token_turns("q0")
            pe.wait_ge(tt_out, TURN0["ki"] + 1)
            pe.wait_ge(part_out, NT + 3)
            pe.wait_ge(pad_set, 3)
            for b in range(1, NT):
                for h in range(IH):
                    n = IH * (b - 1) + h
                    if n >= 2:
                        pe.wait_ge(id_relu, n - 1)
                    pe.matmul(banks[:, 6 + n % 2, 0:mask_cols[b]], qiT[:, h // 2, b * P:(b + 1) * P],
                              (kiT, kiT_low)[h % 2][:, 0:mask_cols[b]], start=True, stop=True).then_inc(id_done, 1)
            def channel_products(first, count):
                with pe.Fori(0, count // 4) as tt:
                    t = tt * 4
                    for s in range(4):
                        n = first + s
                        pe.wait_ge(w_ready, t + (U_CHAN + n + 1))
                        pe.wait_ge(cp_out, t + (n + 1))
                        wh, wl = unit_parts(U_CHAN + n, KC)
                        for k in range(KC):
                            ins = split_product(banks[:, n % 4, :], (wh[:, k, :], wl[:, k, :]), (x_hi[:, k, :], xn_lo[:, k, :]),
                                                k == 0, k == KC - 1)
                        ins.then_inc(w_used, 1)

            pe.wait_ge(tp_out, NT * len(TOK_KINDS))
            channel_products(0, 20)
            token_turns("q1")
            channel_products(20, 4)
            pe.wait_ge(tt_out, TURN0["end"])
            for t in range(2):
                for h in range(4 * t, 4 * t + 4):
                    ins = pe.matmul(banks[:, 4 + t, h % 4 * P:(h % 4 + 1) * P], qT[:, h, 0:P], kT[:, t, 0:P], start=True, stop=True)
                ins.then_inc(s_done, 4)
            channel_products(24, 8)
            pe.wait_ge(id_relu, IH * (NT - 1))
            for t in range(2):
                pe.wait_ge(s_prob, 4 * t + 4)
                for h in range(4):
                    ins = pe.transpose(banks[:, 6 + t, h * P:(h + 1) * P], probs_first[:, t, h * P:(h + 1) * P], ident)
                ins.then_inc(p_turned, 4)
            channel_products(32, 4)
            for t in range(2):
                pe.wait_ge(p_out, 4 * t + 4)
                pe.matmul(banks[:, 4 + t, :], v_tok[:, 0, t * HD:(t + 1) * HD], probsT_first[:, t, :],
                          start=True, stop=True).then_inc(o_done, 4)
            channel_products(36, 4)
            def att_scores(n):
                b, h = divmod(n, HEADS)
                if n >= 2:
                    pe.wait_ge(s_max, n - 1)
                pe.matmul(banks[:, n % 2, 0:mask_cols[b]], qT[:, h, b * P:(b + 1) * P],
                          kT[:, h // GROUP, 0:mask_cols[b]], start=True, stop=True).then_inc(s_done, 1)

            def att_turn(n, probs, bank):
                pe.wait_ge(s_prob, n + 1)
                if n >= 2:
                    pe.wait_ge(p_out, n - 1)
                for c in range(n // HEADS + 1):
                    ins = pe.transpose(banks[:, bank, c * P:(c + 1) * P], probs[:, c * P:(c + 1) * P], ident)
                ins.then_inc(p_turned, 1)

            def att_values(n, probsT, acc, merged):
                b, h = divmod(n, HEADS)
                pe.wait_ge(p_out, n + 1)
                if merged > 0:
                    pe.wait_ge(o_used, merged)
                for c in range(b + 1):
                    ins = pe.matmul(acc, v_tok[:, c, h // GROUP * HD:(h // GROUP + 1) * HD],
                                    probsT[:, c * P:(c + 1) * P], start=(c == 0), stop=(c == b))
                ins.then_inc(o_done, 1)

            def out_unit(u, q, blocks, bank):
                if U_OUT + WSLOTS <= u < U_QUERY:
                    pe.wait_ge(w_ready0, u - U_OUT - WSLOTS + 1)
                else:
                    pe.wait_ge(w_ready, lo_parts(u))
                wh, wl = unit_parts(u, 2)
                for n, b in enumerate(blocks):
                    tb = slice(b * P, (b + 1) * P)
                    for c in range(2):
                        k = 2 * q + c
                        ins = split_product(banks[:, bank[n], :], (x_hi[:, k, tb], mixed_lo[:, k, tb]),
                                            (wh[:, c, :], wl[:, c, :]), k == 0, k == KC - 1)
                ins.then_inc(w_used, 1)

            for q in range(8):
                if q in (0, 2):
                    pe.wait_ge(m_ready0[q // 2], 1)
                out_unit(U_OUT + q, q % 4, [0], [6 + q // 4])
            turn_block(xn0, NT + 1, 2 * NT, 4)
            pe.wait_ge(n_out, 2 * NT + 2)
            pe.wait_ge(key_in, 16)
            for j in range(2 * PH + 2):
                if j < 2 * PH:
                    u = U_QUERY + j
                    pe.wait_ge(w_in[u % WSLOTS], 16 * (u // WSLOTS))
                    if j >= 4:
                        pe.wait_ge(q_out, j - 3)
                    w = slot_of(u)[0].rearrange("p (k c) -> p k c", k=KC)
                    for k in range(KC):
                        ins = pe.matmul(banks[:, j % 4, 0:P], w[:, k, :], hn0[:, k, :], start=(k == 0), stop=(k == KC - 1))
                    ins.then_inc(w_used, 1)
                if j >= 2:
                    h, a = divmod(j - 2, 2)
                    pe.wait_ge(q_out, j - 1)
                    if h >= 4 and a == 0:
                        pe.wait_ge(k_out, h - 3)
                    ins = pe.matmul(banks[:, 4 + h % 4, a * P:(a + 1) * P], q2T0[:, (j - 2) % 4, :], key0[:, j - 2, :],
                                    start=True, stop=True)
                    if a == 1:
                        ins.then_inc(k_done, 1)

            def side(g):
                ga = g - G_ATT
                for j in range(2):
                    n = HEADS + 2 * ga - 4 + j
                    if HEADS <= n < UNITS:
                        att_turn(n, probs_side[:, n % 4, :], 2 + j)
                    n = HEADS + 2 * ga + j
                    if n < UNITS:
                        att_scores(n)
                for j in range(2):
                    n = HEADS + 2 * ga - 6 + j
                    if HEADS <= n < UNITS:
                        att_values(n, probsT_side[:, j, :], banks[:, 6, j * P:(j + 1) * P], n - j)
                if G_OUT <= g < G_OUT + 4:
                    if g == G_OUT:
                        pe.wait_ge(m_ready, NT - 1)
                        pe.wait_ge(o_used, UNITS)
                    for q in range(2 * (g - G_OUT), 2 * (g - G_OUT) + 2):
                        out_unit(U_OUT2 + q, q % 4, [1, 2, 3], ([0, 1, 2], [3, 6, 7])[q // 4])
                if g == G_NORM:
                    for b, bank in ((1, 0), (2, 2), (3, 6)):
                        turn_block(xn_tok[:, b, :], NT + 1 + b, 2 * NT + 2 * b, bank)

            def side_query(r, h, a):
                if isinstance(r, int) and h + a == 0:
                    pe.wait_ge(x_ready, 4 * NT - 2)
                pe.wait_ge(w_ready, 2 * r + lo_parts(U_QUERY2 + 2 * h + a))
                pe.wait_ge(q_out, 2 * r + (2 * PH + 2 * h + a - 1))
                wh, wl = unit_parts(U_QUERY2 + a, KC)
                for k in range(KC):
                    ins = split_product(banks[:, a, 0:SB], (wh[:, k, :], wl[:, k, :]), (x_hi[:, k, P:], hn_lo[:, k, P:]),
                                        k == 0, k == KC - 1)
                ins.then_inc(w_used, 1)

            def side_keyscore(r, h, a):
                if a == 0:
                    pe.wait_ge(key2_in[h % 2], 8 * r + 16 * (h // 2 + 1))
                pe.wait_ge(q_out, 2 * r + (2 * PH + 2 * h + a + 1))
                pe.wait_ge(k_out, 2 * r + (PH + 2 * h + a - 1))
                for b in range(NT - 1):
                    ins = pe.matmul(banks[:, 2 + a, b * P:(b + 1) * P], q2T[:, a, b * P:(b + 1) * P],
                                    key_sb[:, h % 2, a * NKEY:(a + 1) * NKEY], start=True, stop=True)
                ins.then_inc(k_done, 1)

            def experts(r, i):
                late = i >= I_QUERY
                pair = i % 2 if late else 0
                pe.wait_ge(acc_free, r + (i + (1 if i > I_QUERY else 2)))
                for k in range(PTOP):
                    pe.wait_ge(diag_done, r * PTOP + (i * PTOP + k + 1))
                    for s in range(2):
                        ins = pe.matmul(banks[:, 4 + 2 * pair + s, :], diag[:, k % DIAGS, :],
                                        slots[:, slot(k), D + s * 512:D + (s + 1) * 512],
                                        start=(k == 0), stop=(k == PTOP - 1))
                    ins.then_inc(row_free, 1)
                    if k % 4 == 3:
                        q = k // 4
                        if i < I_QUERY:
                            side(4 * i + q)
                        elif i < I_QUERY + PH:
                            h = i - I_QUERY
                            if q in (1, 2):
                                side_keyscore(r, h, q - 1)
                            if q in (0, 1):
                                side_query(r, h, q)

            for_all_iterations(pe, experts)
        @block.scalar
        def _(act):
            def split_weights(r, u):
                if U_OUT + WSLOTS <= u < U_QUERY:
                    act.wait_ge(wo0_in[u - U_OUT - WSLOTS], 16)
                else:
                    act.wait_ge(w_in[u % WSLOTS], r + 16 * (u // WSLOTS + 1))
                if not isinstance(r, int):
                    act.nop(nofuse=True)
                full, (hi, lo) = slot_of(u)
                act.activation(hi, full, ACT.Copy).then_inc(w_split, 1)

            def split_norm(blocks, full):
                for b in blocks:
                    for j in range(2):
                        act.wait_ge(n_out, 2 * b + j + (1 if full is xn_block else 2 * NT + 1))
                        act.activation(x_hi[:, 4 * j:4 * j + 4, b * P:(b + 1) * P], full(b)[:, 4 * j:4 * j + 4, :],
                                       ACT.Copy).then_inc(x_split, 1)

            def squares(n, b, col, junk):
                if n >= 1:
                    act.wait_ge(n_sq, n)
                act.activation(junk, resid[:, b, :], ACT.Square, accum_out=st[:, 0, col:col + 1]).then_inc(n_sq, 1)

            def root(n, at, cols):
                act.wait_ge(n_var, n + 1)
                act.activation(st[:, 2, at:at + cols], st[:, 1, at:at + cols], ACT.Sqrt).then_inc(n_root, 1)

            for b in range(NT):
                act.wait_ge(x_in[b], 16)
                squares(b, b, b, square)
                root(b, b, 1)
            for b in range(NT):
                split_norm([b], xn_block)
                split_weights(0, b)

            def copy_out(g):
                split_weights(0, TOK_START[g] + WSLOTS)
                if g >= 2:
                    root(NT + g - 2, 0, (8, 16)[g - 2])
                split_weights(0, TOK_START[g] + WSLOTS + 1)
                split_weights(0, TOK_START[g] + WSLOTS + 2)
                for b in range(NT):
                    n = NT * g + b
                    if b < NT - 1:
                        act.wait_ge(tp_done, (NT - 1) * g + b + 1)
                    else:
                        act.wait_ge(w_used, TOK_START[g] + 4)
                    if b == 0 and g >= 2:
                        act.wait_ge(tt_done, TURN0[TOK_KINDS[g - 2]] + TURNS[TOK_KINDS[g - 2]])
                    if g == 0 and b == 0:
                        act.wait_ge(n_sq, NT)
                    if TOK_KINDS[g] == "kv":
                        act.activation(raws[:, g % 2, b, 0:256], banks[:, b, 0:256], ACT.Copy).then_inc(part_out, 1)
                        act.activation(v_tok[:, b, :], banks[:, b, 256:512], ACT.Copy).then_inc(tp_out, 1)
                    else:
                        act.activation(raws[:, g % 2, b, :], banks[:, b, :], ACT.Copy).then_inc(tp_out, 1)

            def turns_out(kind):
                for j in range(TURNS[kind]):
                    m = TURN0[kind] + j
                    act.wait_ge(tt_done, m + 1)
                    if kind == "ki":
                        act.activation(kiT[0:64], banks[0:64, 4 + m % 2, :], ACT.Copy).then_inc(part_out, 1)
                        act.activation(kiT_low[64:P], banks[64:P, 4 + m % 2, :], ACT.Copy).then_inc(tt_out, 1)
                        continue
                    dst = {"q0": qT[:, j, :], "q1": qT[:, 4 + j, :], "kv": kT[:, j % 2, :], "qi": qiT[:, j, :]}[kind]
                    act.activation(dst, banks[:, 4 + m % 2, :], ACT.Copy).then_inc(tt_out, 1)

            act.nop(nofuse=True).then_inc(cp_out, 4)
            for g, kind in enumerate(TOK_KINDS):
                copy_out(g)
                if g >= 1:
                    turns_out(TOK_KINDS[g - 1])
                if kind == "kv":
                    act.wait_ge(ki_back, 1)
                    back = banks[:, 7, :].rearrange("p (b c) -> p b c", b=NT)
                    act.activation(ki_raw[:, :, 0:ID], back[:, :, 0:ID], ACT.Copy).then_inc(part_out, 1)
                    act.activation(ki_raw[:, :, ID:2 * ID], back[:, :, 0:ID], ACT.Copy).then_inc(part_out, 1)
                    act.activation(wi, back[:, :, ID:ID + IH], ACT.Copy, scale=IDX_W_SCALE).then_inc(ki_tok, 1)
                if kind == "q0":
                    turns_out("ki")
                split_weights(0, TOK_START[g] + WSLOTS + 3)
                if kind == "qi":
                    act.wait_ge(w_used, U_KI + 1)
                    act.activation(ki_chan, banks[:, 6, :], ACT.Copy).then_inc(ki_out, 1)
                    split_weights(0, U_KI + WSLOTS)
            for b in range(1, NT):
                for h in range(IH):
                    n = IH * (b - 1) + h
                    act.wait_ge(id_done, n + 1)
                    if n >= 2:
                        act.wait_ge(id_used, n - 1)
                    act.activation(relus[:, n % 2, 0:mask_cols[b]], banks[:, 6 + n % 2, 0:mask_cols[b]],
                                   ACT.Relu, scale=IDX_SCALE).then_inc(id_relu, 1)
            root(NT + 2, 0, 16)
            act.wait_ge(n_scaled, NT)
            act.wait_ge(n_turned, 2 * NT)
            def split_mixed(b, h0, h1):
                act.wait_ge(o_used, HEADS * b + h1)
                tb = slice(b * P, (b + 1) * P)
                act.activation(x_hi[:, h0:h1, tb], mixed[:, h0:h1, tb], ACT.Copy).then_inc(m_split, 1)

            for n in range(5 * KC):
                m, q = divmod(n, 5)
                act.wait_ge(w_used, U_CHAN + n + 1)
                if q == 0:
                    act.wait_ge(cv_done, m + 1)
                dst = chan_sets[:, m % 4, q, :] if q < 4 else gate_b[:, m, :]
                act.activation(dst, banks[:, n % 4, :], ACT.Copy if q < 3 else ACT.Sigmoid).then_inc(cp_out, 1)
                if n == 19:
                    turns_out("q1")
                if n == 27:
                    for t in range(2):
                        act.wait_ge(s_max, 4 * t + 4)
                        act.activation(probs_first[:, t, :], probs_first[:, t, :], ACT.Exp, scale=ATTN_SCALE).then_inc(s_exp, 4)
                if n == 33:
                    for t in range(2):
                        act.wait_ge(p_turned, 4 * t + 4)
                        act.activation(probsT_first[:, t, :], banks[:, 6 + t, :], ACT.Copy).then_inc(p_out, 4)
                if n == 5 * KC - 1:
                    split_mixed(0, 0, 4)
                split_weights(0, U_CHAN + n + WSLOTS)


            def att_exp(n, probs):
                act.wait_ge(s_max, n + 1)
                act.activation(probs[:, 0:mask_cols[n // HEADS]], probs[:, 0:mask_cols[n // HEADS]], ACT.Exp,
                               bias=sm[:, n % 4, 1:2], scale=ATTN_SCALE, accum_out=sm[:, n % 4, 2:3]).then_inc(s_exp, 1)

            def att_scale(n, probs):
                act.wait_ge(s_inv, n - HEADS + 1)
                act.activation(probs[:, 0:mask_cols[n // HEADS]], probs[:, 0:mask_cols[n // HEADS]], ACT.Copy,
                               scale=sm[:, n % 4, 3:4]).then_inc(s_prob, 1)

            def att_turned(n, probsT, bank):
                act.wait_ge(p_turned, n + 1)
                if n >= 2:
                    act.wait_ge(o_done, n - 1)
                cols = mask_cols[n // HEADS]
                act.activation(probsT[:, 0:cols], banks[:, bank, 0:cols], ACT.Copy).then_inc(p_out, 1)

            split_mixed(0, 4, HEADS)
            for u in range(U_OUT + WSLOTS, U_QUERY):
                split_weights(0, u)
            act.wait_ge(y_out, 2)
            squares(NT, 0, 0, square)
            root(NT + 3, 0, 1)
            for j in range(2 * PH):
                act.wait_ge(w_used, U_QUERY + j + 1)
                if j >= 4:
                    act.wait_ge(k_done, (j - 4) // 2 + 1)
                act.activation(q2T0[:, j % 4, :], banks[:, j % 4, 0:P], ACT.Copy).then_inc(q_out, 1)
                if j == 3:
                    act.wait_ge(k_out, 1)
                    act.activation(sc.rearrange("p a n -> p (a n)"), scores[:, 0:2 * NKEY], ACT.Copy).then_inc(r_in, 1)
                if j == 9:
                    act.wait_ge(r_max, 1)
                    act.activation(gprob[:, 0, :], best, ACT.Exp, bias=gstat[:, 0:1], accum_out=gstat[:, 1:2]).then_inc(r_exp, 1)

            def split_weights2(r, u, loaded, n):
                act.wait_ge(loaded, r * 16 + 16 * (n + 1))
                if not isinstance(r, int):
                    act.nop(nofuse=True)
                full, (hi, lo) = slot_of(u)
                act.activation(hi, full, ACT.Copy).then_inc(w_split, 1)

            def side(g):
                ga = g - G_ATT
                for j in range(2):
                    n = HEADS + 2 * ga - 6 + j
                    if HEADS <= n < UNITS:
                        att_turned(n, probsT_side[:, j, :], 2 + j)
                for j in range(2):
                    n = HEADS + 2 * ga - 4 + j
                    if HEADS <= n < UNITS:
                        att_scale(n, probs_side[:, n % 4, :])
                for j in range(2):
                    n = HEADS + 2 * ga - 2 + j
                    if HEADS <= n < UNITS:
                        att_exp(n, probs_side[:, n % 4, :])
                for b in range(1, NT):
                    if ga == 4 * b + 3:
                        split_mixed(b, 0, HEADS)
                for q in OUT_SPLITS.get(g, ()):
                    split_weights2(0, U_OUT2 + q, wo2_in[q % 4], q // 4)
                if g == G_ADD + 1:
                    act.wait_ge(y_out, 2 * NT)
                    for b in range(1, NT):
                        squares(NT + b, b, b - 1, square2)
                if g == G_NORM:
                    root(NT + 4, 0, NT - 1)
                if g == G_NORM + 1:
                    split_norm(range(1, NT), hn_block)

            def side_query_out(r, h, a):
                act.wait_ge(w_used, 2 * r + (U_QUERY2 + 2 * h + a + 1))
                act.wait_ge(k_done, 2 * r + (PH + 2 * h + a - 1))
                if not isinstance(r, int):
                    act.nop(nofuse=True)
                act.activation(q2T[:, a, :], banks[:, a, 0:SB], ACT.Copy).then_inc(q_out, 1)

            act.wait_ge(k_out, PH)
            act.wait_ge(xn_ready, 1)
            act.wait_ge(pad_set, 1)

            def experts(r, i):
                act.wait_ge(r_done, r + (i + 1))
                if PH - 1 <= i <= I_QUERY + PH:
                    act.wait_ge(k_out, 2 * r + (PH + 2 * (i + 1 - PH) + 2))
                act.nop(nofuse=True)
                act.activation(sc.rearrange("p a n -> p (a n)"),
                               scores[:, (i + 1) * 2 * NKEY:(i + 2) * 2 * NKEY] if isinstance(r, int) else
                               scores[:, bass.ds((r + (i + 1)) * (2 * NKEY), 2 * NKEY)], ACT.Copy).then_inc(r_in, 1)
                for q in range(4):
                    for ks in gelu_groups(i, q):
                        act.wait_ge(dot_done, r * PTOP + (i * PTOP + ks[-1] + 1))
                        act.activation(gel[:, ks[0]:ks[-1] + 1], dots[:, ks[0]:ks[-1] + 1], ACT.Gelu).then_inc(gel_done, 1)
                    if q == 1:
                        act.wait_ge(r_max, r + (i + 2))
                        act.activation(gprob[:, (i + 1) % 2, :], best, ACT.Exp, bias=gstat[:, 0:1],
                                       accum_out=gstat[:, 1:2]).then_inc(r_exp, 1)
                    if i < I_QUERY:
                        side(4 * i + q)
                    elif i < I_QUERY + PH:
                        h = i - I_QUERY
                        if q in (1, 2):
                            side_query_out(r, h, q - 1)
                        if q in (0, 1):
                            split_weights2(r, U_QUERY2 + q, wq2_in[q], h)

            for_all_iterations(act, experts)

        @block.gpsimd
        def _(pool):
            pool.memset(scores[:, ITERS * 2 * NKEY:], 0.0).then_inc(pad_set, 1)
            pool.wait_ge(pad_set, 1)
            pool.memset(kiT[64:P], 0.0).then_inc(pad_set, 1)
            pool.wait_ge(pad_set, 2)
            pool.memset(kiT_low[0:64], 0.0).then_inc(pad_set, 1)

            pool.wait_ge(pad_set, 3)

            def rest_of_weights(t, u):
                pool.wait_ge(w_split, t + splits(u))
                full, (hi, lo) = slot_of(u)
                pool.tensor_tensor(lo, full, hi.bitcast(F32), ALU.subtract).then_inc(w_ready, 1)

            def rest_of_weight_loop(first, count):
                with pool.Fori(0, count // WSLOTS) as tt:
                    for s in range(WSLOTS):
                        rest_of_weights(tt * WSLOTS, first + s)

            def rest_of_norm():
                for b in range(1, NT):
                    for j in range(2):
                        pool.wait_ge(x_split, 2 * NT - 2 + 2 * b + j + 1)
                        piece = (slice(None), slice(4 * j, 4 * j + 4), slice(b * P, (b + 1) * P))
                        pool.tensor_tensor(hn_lo[piece], hn_full[piece], x_hi[piece].bitcast(F32), ALU.subtract).then_inc(x_ready, 1)

            def rest_of_mixed(b):
                pool.wait_ge(m_split, b + 2)
                tb = slice(b * P, (b + 1) * P)
                pool.tensor_tensor(mixed_lo[:, :, tb], mixed[:, :, tb], x_hi[:, :, tb].bitcast(F32), ALU.subtract).then_inc(m_ready, 1)

            for u in range(WSLOTS):
                rest_of_weights(0, u)
            rest_of_weight_loop(WSLOTS, U_OUT - 1)
            pool.wait_ge(m_split, 1)
            pool.tensor_tensor(mixed_lo[:, 0:4, 0:P], mixed[:, 0:4, 0:P], x_hi[:, 0:4, 0:P].bitcast(F32),
                               ALU.subtract).then_inc(m_ready0[0], 1)
            rest_of_weights(0, U_OUT + WSLOTS - 1)
            pool.wait_ge(g2row_in, 16)
            pool.wait_ge(n_turned, 2 * NT + 2)
            pool.tensor_tensor(xn0, xn0, g2row0, ALU.mult).then_inc(xn_ready, 1)

            def side(g):
                for b in range(1, NT):
                    if g - G_ATT == 4 * b + 4:
                        rest_of_mixed(b)
                for q in OUT_SPLITS.get(g, ()):
                    rest_of_weights(0, U_OUT2 + q)
                if g == G_NORM + 2:
                    rest_of_norm()
                if g == G_GAIN:
                    pool.wait_ge(g2again_in, 16)
                    for b in range(1, NT):
                        pool.wait_ge(n_turned, 2 * NT + 2 * b + 2)
                        pool.tensor_tensor(xn_tok[:, b, :], xn_tok[:, b, :], g2row, ALU.mult).then_inc(xn_ready, 1)

            pool.wait_ge(w_used, U_QUERY)
            pool.wait_ge(cv_done, 4 + KC)

            def experts(r, i):
                pool.wait_ge(r_done, r + (i + 1))
                for k in range(PTOP):
                    if i == 0 and k == 3:
                        pool.wait_ge(k_done, PH)
                        pool.wait_ge(xn_ready, 1)
                    pool.wait_ge(row_free, r * PTOP + (i * PTOP + k + 1))
                    pool.nop(nofuse=True)
                    pool.indirect_dma_start(slots[:, slot(k), :], None, uv,
                                            bass.IndirectOffsetOnAxis(eidx[:, i % 2, k:k + 1], 0)).then_inc(row_in[slot(k)], 16)
                    if k % 4 == 3:
                        q = k // 4
                        if 0 <= 4 * i + q - 1 < 4 * I_QUERY:
                            side(4 * i + q - 1)
                        if I_QUERY <= i < I_QUERY + PH and q in (1, 2):
                            u = U_QUERY2 + 2 * (i - I_QUERY) + q - 1
                            pool.wait_ge(w_split, 2 * r + splits(u))
                            full, (hi, lo) = query_slots[q - 1]
                            pool.tensor_tensor(lo, full, hi.bitcast(F32), ALU.subtract).then_inc(w_ready, 1)

            for_all_iterations(pool, experts)

        @block.vector
        def _(dve):
            link = Link(dve, ch_dve)
            dve.nop(nofuse=True).then_inc(cv_done, 4)
            dve.wait_ge(const_in, 64)

            def inv_root(n, at, cols, width):
                dve.tensor_scalar(st[:, 1, at:at + cols], st[:, 0, at:at + cols], 1.0 / width, EPS, ALU.mult, ALU.add).then_inc(n_var, 1)
                dve.wait_ge(n_root, n + 1)
                link.then(dve.reciprocal(st[:, 3, at:at + cols], st[:, 2, at:at + cols]))
                link.then(dve.tensor_tensor(st[:, 4, at:at + cols], st[:, 3, at:at + cols], st[:, 3, at:at + cols], ALU.mult))
                link.then(dve.tensor_tensor(st[:, 4, at:at + cols], st[:, 4, at:at + cols], st[:, 1, at:at + cols], ALU.mult))
                link.then(dve.tensor_scalar(st[:, 4, at:at + cols], st[:, 4, at:at + cols], -0.5, 1.5, ALU.mult, ALU.add))
                link.then(dve.tensor_tensor(st[:, 3, at:at + cols], st[:, 3, at:at + cols], st[:, 4, at:at + cols], ALU.mult))

            def norm_scale(b, col, dst):
                dve.tensor_scalar(dst, resid[:, b, :], st[:, 3, col:col + 1], None, ALU.mult).then_inc(n_scaled, 1)

            def norm_out(m0, full, gain, bank):
                for j in range(2):
                    dve.wait_ge(n_turned, m0 + j + 1)
                    dve.tensor_tensor(full[:, 4 * j:4 * j + 4, :], banks[:, bank + j, :].rearrange("p (c t) -> p c t", c=4),
                                      gain[:, 4 * j:4 * j + 4].unsqueeze(2).to_broadcast([P, 4, P]), ALU.mult).then_inc(n_out, 1)

            for b in range(NT):
                dve.wait_ge(n_sq, b + 1)
                inv_root(b, b, 1, D)
                norm_scale(b, b, xn_tok[:, b, :])
            dve.wait_ge(n_scaled, NT)
            for b in range(NT + 1):
                if b < NT:
                    norm_out(2 * b, xn_block(b), g1, 4)
                for j in range(2 if b >= 1 else 0):
                    dve.wait_ge(x_split, 2 * (b - 1) + j + 1)
                    piece = (slice(None), slice(4 * j, 4 * j + 4), slice((b - 1) * P, b * P))
                    dve.tensor_tensor(xn_lo[piece], xn_full[piece], x_hi[piece].bitcast(F32), ALU.subtract).then_inc(x_ready, 1)

            def rotate(x1, x2, cos, sin, shape):
                n = shape[1] * shape[2] * shape[3]
                c, s_ = (t.unsqueeze(2).to_broadcast(shape) for t in (cos, sin))
                tv = [turn[:, q, 0:n].rearrange("p (b h r) -> p b h r", b=shape[1], h=shape[2]) for q in range(4)]
                link(dve.tensor_tensor(tv[0], x1, c, ALU.mult))
                link(dve.tensor_tensor(tv[1], x2, s_, ALU.mult))
                link(dve.tensor_tensor(tv[2], x2, c, ALU.mult))
                link.then(dve.tensor_tensor(tv[3], x1, s_, ALU.mult))
                link(dve.tensor_tensor(x1, tv[0], tv[1], ALU.subtract))
                dve.tensor_tensor(x2, tv[2], tv[3], ALU.add).then_inc(tp_ready, 1)
                link.upto(link.count)

            def token_group(kind):
                g = TOK_KINDS.index(kind) if kind in TOK_KINDS else None
                if kind == "ki":
                    dve.wait_ge(part_out, NT + 2)
                    dve.wait_ge(ki_tok, 1)
                else:
                    dve.wait_ge(tp_out, NT * (g + 1))
                if kind == "kv":
                    dve.wait_ge(part_out, NT)
                if kind != "qi":
                    dve.wait_ge(tp_ready, list(TURNS).index(kind))
                if kind in ("kv", "q0", "q1"):
                    nh, gain = (2, 1) if kind == "kv" else (4, 0)
                    cols = NT * nh
                    r4 = raws[:, g % 2, :, 0:nh * HD].rearrange("p b (h c) -> p b h c", h=nh)
                    sq = head_sq[:, 0:cols * HD].rearrange("p (b h c) -> p b h c", b=NT, h=nh)
                    link.then(dve.tensor_tensor(sq, r4, r4, ALU.mult))
                    link.then(dve.tensor_reduce(st[:, 0, 0:cols], head_sq[:, 0:cols * HD].rearrange("p (n c) -> p n c", c=HD),
                                                AX.X, ALU.add))
                    inv_root(NT + g - 1, 0, cols, HD)
                    inv = st[:, 3, 0:cols].rearrange("p (b h) -> p b h", b=NT)
                    for b in range(NT):
                        rb = r4[:, b, :, :]
                        link(dve.tensor_tensor(rb, rb, inv[:, b, :].unsqueeze(2).to_broadcast([P, nh, HD]), ALU.mult))
                    link.upto(link.count)
                    for b in range(NT):
                        rb = r4[:, b, :, :]
                        link(dve.tensor_tensor(rb, rb, qk_gain[:, gain, :].unsqueeze(1).to_broadcast([P, nh, HD]), ALU.mult))
                    link.upto(link.count)
                    rotate(r4[:, :, :, 0:ROPE_Q], r4[:, :, :, ROPE_Q:2 * ROPE_Q], cos_q, sin_q, [P, NT, nh, ROPE_Q])
                else:
                    nh = IH if kind == "qi" else 2
                    r4 = (ki_raw if kind == "ki" else raws[:, g % 2, :, :]).rearrange("p b (h c) -> p b h c", h=nh)
                    rotate(r4[:, :, :, 0:ROPE_I], r4[:, :, :, ROPE_I:2 * ROPE_I], cos_i, sin_i, [P, NT, nh, ROPE_I])

            for kind in ("qi", "kv", "ki", "q0"):
                token_group(kind)

            for b in range(1, NT):
                for h in range(IH):
                    n = IH * (b - 1) + h
                    dve.wait_ge(id_relu, n + 1)
                    r = relus[:, n % 2, 0:mask_cols[b]]
                    if h == 0:
                        dve.tensor_scalar(masks[b], r, wi[:, b, 0:1], None, ALU.mult).then_inc(id_used, 1)
                    else:
                        dve.wait_ge(id_used, n)
                        dve.scalar_tensor_tensor(masks[b], r, wi[:, b, h:h + 1], masks[b], ALU.mult, ALU.add).then_inc(id_used, 1)
                dve.wait_ge(id_used, IH * b)
                link(dve.tensor_tensor(masks[b][:, b * P:], masks[b][:, b * P:], tri, ALU.add))
            link.upto(link.count)
            token_group("q1")
            def short_conv(m):
                dve.wait_ge(cp_out, 4 + 5 * m + 4)
                u, part4 = u_pad[:, m % 2, :], chan_sets[:, m % 4, :, :]
                link.then(dve.tensor_tensor(u[:, CONV_K - 1:], part4[:, 0, :], part4[:, 1, :], ALU.mult))
                link.then(dve.tensor_scalar(conv, u[:, 0:SEQ], taps[:, m, 0:1], None, ALU.mult))
                for j in range(1, CONV_K):
                    link.then(dve.scalar_tensor_tensor(conv, u[:, j:j + SEQ], taps[:, m, j:j + 1], conv, ALU.mult, ALU.add))
                link.then(dve.tensor_tensor(conv, conv, part4[:, 2, :], ALU.mult))
                dve.tensor_tensor(mixed[:, m, :], conv, part4[:, 3, :], ALU.mult).then_inc(cv_done, 1)
                dve.wait_ge(cv_done, 4 + m + 1)

            for b in range(1, NT):
                if b == NT - 1:
                    dve.wait_ge(tt_done, TURN0["q1"])
                    link.then(dve.memset(u_pad[:, :, 0:CONV_K - 1], 0.0))
                    short_conv(0)
                for _ in range(TOPK_KEYS // 8):
                    link.then(dve.max(mx8, masks[b]))
                    link.then(dve.match_replace(masks[b], mx8, masks[b], TAKEN))
                link.then(dve.tensor_scalar(masks[b], masks[b], TAKEN / 2, MASKED, ALU.is_gt, ALU.mult))

            def att_max(n, probs, free):
                b = n // HEADS
                dve.wait_ge(s_done, n + 1)
                if free > 0:
                    dve.wait_ge(p_turned, free)
                cols = mask_cols[b]
                link.then(dve.tensor_tensor_reduce(out=probs[:, 0:cols], in0=banks[:, n % 2, 0:cols], in1=tri if b == 0 else masks[b],
                                                   scale=1.0, scalar=TAKEN, op0=ALU.add, op1=ALU.max,
                                                   accum_out=sm[:, n % 4, 0:1]))
                dve.tensor_scalar(sm[:, n % 4, 1:2], sm[:, n % 4, 0:1], -ATTN_SCALE, None, ALU.mult).then_inc(s_max, 1)

            def att_inverse(n):
                dve.wait_ge(s_exp, n + 2)
                pair = sm[:, n % 4:n % 4 + 2, :]
                dve.reciprocal(pair[:, :, 3], pair[:, :, 2]).then_inc(s_inv, 2)

            def att_merge(n):
                b, h = divmod(n, HEADS)
                dve.wait_ge(o_done, n + 2)
                gate, sofar = (t[:, h:h + 2, b * P:(b + 1) * P] for t in (gate_b, mixed))
                link.then(dve.tensor_tensor(gate, banks[:, 6, 0:2 * P].rearrange("p (h n) -> p h n", h=2), gate, ALU.mult))
                dve.tensor_tensor(sofar, sofar, gate, ALU.add).then_inc(o_used, 2)

            four = [probs_first[:, t, :].rearrange("p (h n) -> p h n", h=4) for t in range(2)]
            stat = [[st[:, a, 4 * t:4 * t + 4] for a in range(3)] for t in range(2)]

            def heads_of(ap, t):
                return ap[:, 4 * t:4 * t + 4, 0:P]

            for m in range(1, 5):
                short_conv(m)
            for t in range(2):
                dve.wait_ge(s_done, 4 * t + 4)
                link.then(dve.tensor_tensor(four[t], banks[:, 4 + t, :].rearrange("p (h n) -> p h n", h=4),
                                            tri.unsqueeze(1).to_broadcast([P, 4, P]), ALU.add))
                link.then(dve.tensor_reduce(stat[t][0], four[t], AX.X, ALU.max))
                dve.tensor_tensor(four[t], four[t], stat[t][0].unsqueeze(2).to_broadcast([P, 4, P]), ALU.subtract).then_inc(s_max, 4)
            for t in range(2):
                dve.wait_ge(s_exp, 4 * t + 4)
                link.then(dve.tensor_reduce(stat[t][1], four[t], AX.X, ALU.add))
                link.then(dve.reciprocal(stat[t][2], stat[t][1]))
                dve.tensor_tensor(four[t], four[t], stat[t][2].unsqueeze(2).to_broadcast([P, 4, P]), ALU.mult).then_inc(s_prob, 4)
            def rest_of_weights(u):
                dve.wait_ge(w_split, splits(u))
                full, (hi, lo) = slot_of(u)
                dve.tensor_tensor(lo, full, hi.bitcast(F32), ALU.subtract).then_inc(w_ready0, 1)

            for t in range(2):
                for m in ((5, 6), (7,))[t]:
                    short_conv(m)
                if t == 1:
                    dve.wait_ge(cp_out, 4 + 5 * KC)
                dve.wait_ge(o_done, 4 * t + 4)
                link.then(dve.tensor_tensor(heads_of(gate_b, t), banks[:, 4 + t, :].rearrange("p (h n) -> p h n", h=4),
                                            heads_of(gate_b, t), ALU.mult))
                dve.tensor_tensor(heads_of(mixed, t), heads_of(mixed, t), heads_of(gate_b, t), ALU.add).then_inc(o_used, 4)
            dve.wait_ge(m_split, 2)
            dve.tensor_tensor(heads_of(mixed_lo, 1), heads_of(mixed, 1), heads_of(x_hi, 1).bitcast(F32),
                              ALU.subtract).then_inc(m_ready0[1], 1)
            for u in range(U_OUT + WSLOTS, U_QUERY):
                rest_of_weights(u)

            def add_half(b, s, bank):
                half = resid[:, b, s * 512:(s + 1) * 512]
                dve.tensor_tensor(half, banks[:, bank, :], half, ALU.add).then_inc(y_out, 1)

            dve.wait_ge(x_again, 16)
            for s in range(2):
                dve.wait_ge(w_used, U_OUT + 4 * (s + 1))
                add_half(0, s, 6 + s)
            dve.wait_ge(n_sq, NT + 1)
            inv_root(NT + 3, 0, 1, D)
            norm_scale(0, 0, xn0)
            norm_out(2 * NT, hn0, g2, 4)

            score4 = scores[:, 0:ITERS * 2 * NKEY].rearrange("p (b j n) -> p b j n", b=NT, j=2 * PH)

            def first_scores_out(n):
                dve.wait_ge(k_done, n + 1)
                dve.tensor_copy(scores[:, n * 2 * NKEY:(n + 1) * 2 * NKEY], banks[:, 4 + n % 4, 0:2 * NKEY]).then_inc(k_out, 1)

            first_scores_out(0)

            def side(g):
                ga = g - G_ATT
                n = HEADS + 2 * ga - 4
                if HEADS <= n < UNITS:
                    att_inverse(n)
                for j in range(2):
                    n = HEADS + 2 * ga - 2 + j
                    if HEADS <= n < UNITS:
                        att_max(n, probs_side[:, n % 4, :], n - 3 if n >= HEADS + 4 else 0)
                n = HEADS + 2 * ga - 8
                if HEADS <= n < UNITS:
                    att_merge(n)
                if g in (G_ADD, G_ADD + 1):
                    s = g - G_ADD
                    dve.wait_ge(w_used, U_OUT2 + 4 * (s + 1))
                    for b in range(1, NT):
                        add_half(b, s, ([0, 1, 2], [3, 6, 7])[s][b - 1])
                if g == G_NORM:
                    dve.wait_ge(n_sq, 2 * NT)
                    inv_root(NT + 4, 0, NT - 1, D)
                    for b in range(1, NT):
                        norm_scale(b, b - 1, xn_tok[:, b, :])
                if g == G_NORM + 1:
                    for b, bank in ((1, 0), (2, 2), (3, 6)):
                        norm_out(2 * NT + 2 * b, hn_block(b), g2, bank)

            def side_scores_out(r, h, a):
                dve.wait_ge(k_done, 2 * r + (PH + 2 * h + a + 1))
                j = 2 * h + a
                src = banks[:, 2 + a, 0:SB].rearrange("p (b n) -> p b n", n=NKEY)
                if isinstance(r, int):
                    dst = score4[:, 1:, j, :]
                else:
                    dve.nop(nofuse=True)
                    dst = score4[:, 1:, bass.ds(2 * r + j, 1), :].rearrange("p b a n -> p b (a n)")
                dve.tensor_copy(dst, src).then_inc(k_out, 1)

            def route_keys():
                for a in range(2):
                    ta = link(dve.max(topv[:, a, 0:8], sc[:, a, :]))
                link.upto(ta)
                for a in range(2):
                    link(dve.max_index(topi[:, a, 0:8], topv[:, a, 0:8], sc[:, a, :]))
                    ta = link(dve.match_replace(sc_cut[:, a, :], topv[:, a, 0:8], sc[:, a, :], TAKEN))
                link.upto(ta)
                for a in range(2):
                    ta = link(dve.max(topv[:, a, 8:16], sc_cut[:, a, :]))
                link.upto(ta)
                for a in range(2):
                    ta = link(dve.max_index(topi[:, a, 8:16], topv[:, a, 8:16], sc_cut[:, a, :]))
                link.upto(ta)
                link(dve.tensor_copy(topif, topi))

            def route_pairs():
                link.then(dve.tensor_tensor(cand.rearrange("p (k n) -> p k n", k=PTOP),
                                            topv[:, 0, :].unsqueeze(2).to_broadcast([P, PTOP, PTOP]),
                                            topv[:, 1, :].unsqueeze(1).to_broadcast([P, PTOP, PTOP]), ALU.add))
                link.then(dve.max(best[:, 0:8], cand))
                link(dve.max_index(pos[:, 0:8], best[:, 0:8], cand))
                link.then(dve.match_replace(cand_cut, best[:, 0:8], cand, TAKEN))
                link.then(dve.max(best[:, 8:16], cand_cut))
                link(dve.max_index(pos[:, 8:16], best[:, 8:16], cand_cut))
                dve.tensor_scalar(gstat[:, 0:1], best[:, 0:1], -1.0, None, ALU.mult).then_inc(r_max, 1)
                link.upto(link.count)

            def route_experts(s, exps):
                link(dve.tensor_scalar(posij[:, 0, :], pos, 4, None, ALU.logical_shift_right))
                link.then(dve.tensor_scalar(posij[:, 1, :], pos, 15, None, ALU.bitwise_and))
                link.then(dve.tensor_copy(posf, posij))
                for a in range(2):
                    link(dve.tensor_tensor(onehot[:, a, :, :], posf[:, a, :].unsqueeze(2).to_broadcast([P, PTOP, PTOP]),
                                           iota.unsqueeze(1).to_broadcast([P, PTOP, PTOP]), ALU.is_equal))
                link.upto(link.count)
                for a in range(2):
                    link(dve.tensor_tensor(onehot[:, a, :, :], onehot[:, a, :, :],
                                           topif[:, a, :].unsqueeze(1).to_broadcast([P, PTOP, PTOP]), ALU.mult))
                link.upto(link.count)
                link.then(dve.tensor_reduce(chosen, onehot, AX.X, ALU.add))
                dve.wait_ge(r_exp, exps)
                link(dve.reciprocal(gstat[:, 2:3], gstat[:, 1:2]))
                link.then(dve.scalar_tensor_tensor(eidx[:, s, :], chosen[:, 0, :], float(NKEY), chosen[:, 1, :], ALU.mult, ALU.add))
                dve.tensor_scalar(gprob[:, s, :], gprob[:, s, :], gstat[:, 2:3], None, ALU.mult).then_inc(r_done, 1)

            dve.nop(nofuse=True).then_inc(acc_free, 2)
            dve.wait_ge(r_in, 1)
            route_keys()
            route_pairs()
            route_experts(0, 1)
            link.upto(link.count)
            for n in range(1, PH):
                first_scores_out(n)
            ROUTE_LINKS = 11 + 6 + 10

            def experts(r, i):
                token = xn0 if i < PH else xn_tok[:, i // PH, :]
                if i in (0, PH):
                    dve.wait_ge(xn_ready, NT if i else 1)
                for q in range(4):
                    for n_gelu, ks in enumerate(gelu_groups(i, q)):
                        for k in ks:
                            n = i * PTOP + k
                            dve.wait_ge(row_in[slot(k)], r * 32 + 16 * (2 * i + k // RING + 1))
                            if n >= 2 and k % 4 >= 2 or k == 0 and i >= 1:
                                dve.wait_ge(dot_done, r * PTOP + (n - (1 if k else 0)))
                            dve.tensor_tensor_reduce(out=dotjunk(i, k), in0=slots[:, slot(k), 0:D], in1=token,
                                                     scale=1.0, scalar=0.0, op0=ALU.mult, op1=ALU.add,
                                                     accum_out=dots[:, k:k + 1]).then_inc(dot_done, 1)
                        dve.wait_ge(gel_done, r * 4 + (4 * i + q + n_gelu + 1))
                        if q == 0:
                            dve.wait_ge(r_done, r + (i + 1))
                        for k in ks:
                            n = i * PTOP + k
                            dve.wait_ge(row_free, r * PTOP + (n + 1 + RING - DIAGS))
                            dve.tensor_scalar(diag[:, k % DIAGS, :], ident, gel[:, k:k + 1], gprob[:, i % 2, k:k + 1],
                                              ALU.mult, ALU.mult).then_inc(diag_done, 1)
                    if q == 0:
                        dve.wait_ge(r_in, r + (i + 2))
                        dve.nop(nofuse=True)
                        route_keys()
                    if q == 1:
                        link.upto(link.count)
                        route_pairs()
                        route_experts((i + 1) % 2, r + (i + 2))
                    if i < I_QUERY:
                        side(4 * i + q)
                    elif i < I_QUERY + PH and q >= 2:
                        side_scores_out(r, i - I_QUERY, q - 2)
                dve.wait_ge(row_free, r * PTOP + (PTOP * (i + 1) + RING))
                pair = i % 2 if i >= I_QUERY else 0
                blk = resid[:, i // PH, :].rearrange("p (h c) -> p h c", h=2)
                dve.wait_ge(acc_free, r + (i + 2))
                dve.tensor_tensor(blk, banks[:, 4 + 2 * pair:6 + 2 * pair, :], blk, ALU.add).then_inc(acc_free, 1)

            for_all_iterations(dve, experts, lambda rr: link.enter(rr, 2 * ROUTE_LINKS), link.leave)


def kernel(x, norm1_g, w_in, conv_w, q_norm_g, k_norm_g, w_o, norm2_g, peer_wq, peer_k1, peer_k2, peer_u, peer_v):
    import numpy as np
    import concourse.bacc as bacc
    from concourse.bass_utils import run_bass_kernel_spmd

    a = {k: np.asarray(v) for k, v in dict(
        x=x, norm1_g=norm1_g, w_in=w_in, conv_w=conv_w, q_norm_g=q_norm_g, k_norm_g=k_norm_g, w_o=w_o, norm2_g=norm2_g,
        peer_wq=peer_wq, peer_k1=peer_k1, peer_k2=peer_k2, peer_u=peer_u, peer_v=peer_v).items()}

    def chunks(w, cols):
        n = w.shape[1] // cols
        return np.ascontiguousarray(w.reshape(KC, P, n, cols).transpose(2, 1, 0, 3)).reshape(n, P, KC * cols)

    w = a["w_in"]
    tok = w[:, 3 * D:]
    n_tok = D + 2 * KVH * HD + IH * ID
    small = ID + IH
    ga0 = 3 * D + n_tok + small
    sel = [w[:, D:2 * D], w[:, 2 * D:3 * D], w[:, 0:D], w[:, ga0:ga0 + D], w[:, ga0 + D:ga0 + 2 * D]]
    w_chan = np.stack([chunks(s, P) for s in sel], axis=1).reshape(5 * KC, P, UNIT)

    def halves(w):
        return chunks(w, 512).reshape(-1, P, 4, UNIT).transpose(0, 2, 1, 3).reshape(-1, P, UNIT)

    kv1 = D + 2 * KVH * HD
    padded = np.pad(tok[:, n_tok:n_tok + small], ((0, 0), (0, P - small)))
    w_units = np.concatenate([halves(tok[:, kv1:n_tok]), chunks(padded, P), halves(tok[:, D:kv1]), halves(tok[:, 0:D]), w_chan, halves(a["w_o"]),
                              chunks(a["peer_wq"], P)])

    t = np.arange(SEQ, dtype=np.float32)[:, None]

    def table(fn, half):
        inv = (np.float32(500000.0) ** (-np.arange(half, dtype=np.float32) / np.float32(half))).astype(np.float32)
        v = fn((t * inv[None, :]).astype(np.float32).astype(np.float64)).astype(np.float32)
        return v.reshape(NT, P, half).transpose(1, 0, 2).reshape(P, NT * half)

    lower = np.where(np.arange(P)[None, :] <= np.arange(P)[:, None], 0.0, MASKED).astype(np.float32)
    consts = np.concatenate([np.eye(P, dtype=np.float32), lower, np.tile(np.arange(16, dtype=np.float32), (P, 1)),
                             table(np.cos, ROPE_Q), table(np.sin, ROPE_Q), table(np.cos, ROPE_I), table(np.sin, ROPE_I)], axis=1)
    params = np.concatenate([a["norm1_g"].reshape(KC, P).T, a["norm2_g"].reshape(KC, P).T,
                             a["conv_w"].reshape(CONV_K, KC, P).transpose(2, 1, 0).reshape(P, KC * CONV_K)], axis=1)
    arrays = {
        "x": a["x"].reshape(SEQ, D),
        "w_units": w_units,
        "keys_t": np.ascontiguousarray(np.stack([a["peer_k1"], a["peer_k2"]], axis=1).transpose(0, 1, 3, 2)).reshape(2 * PH, P, NKEY),
        "uv": np.concatenate([a["peer_u"], a["peer_v"]], axis=1),
        "consts": consts,
        "params": params,
        "rows": np.concatenate([a["norm2_g"], a["q_norm_g"], a["k_norm_g"]]),
    }
    arrays = {k: np.ascontiguousarray(v) for k, v in arrays.items()}
    nc = bacc.Bacc("TRN2", target_bir_lowering=False, num_devices=1)
    args = [nc.dram_tensor("in_" + k, v.shape, F32, kind="ExternalInput").ap() for k, v in arrays.items()]
    out = nc.dram_tensor("out_h", (SEQ, D), F32, kind="ExternalOutput").ap()
    build(nc, *args, out)
    r = run_bass_kernel_spmd(nc, [{"in_" + k: v for k, v in arrays.items()}], core_ids=[0])
    return r.results[0]["out_h"].reshape(1, SEQ, D)
```
